# Optimizing a Trainium2 kernel written in Bass

```python
import jax, jax.numpy as jnp
from jax import lax
import numpy as np

D_MODEL = 1024
BATCH = 1
SEQ = 256
DEPTH = 2

CTX_LEN = 256
GRID_W = 64
N_HEADS = 8
N_KV_HEADS = 2
HEAD_DIM = 64
ATTN_W = N_HEADS * HEAD_DIM
KV_W = N_KV_HEADS * HEAD_DIM
CONV_W = D_MODEL - ATTN_W
MIX_W = ATTN_W + CONV_W
IN_W = ATTN_W + 2 * KV_W + 2 * CONV_W
CONV_K = 31
D_FF = 2816
N_EXPERTS = 8
TOP_K = 2
Q_BLOCK = 128
ROPE_THETA = 10000.0
EPS = 1e-6

kernel_name = "hybrid_attn_conformer_moe_prefix_dit"

def rmsnorm(x, g):
    xf = x.astype(jnp.float32)
    y = xf * lax.rsqrt(jnp.mean(xf * xf, axis=-1, keepdims=True) + EPS)
    return (y * g.astype(jnp.float32)).astype(x.dtype)

def layernorm(x, g, b):
    xf = x.astype(jnp.float32)
    mu = jnp.mean(xf, axis=-1, keepdims=True)
    var = jnp.mean(jnp.square(xf - mu), axis=-1, keepdims=True)
    y = (xf - mu) * lax.rsqrt(var + EPS)
    return (y * g.astype(jnp.float32) + b.astype(jnp.float32)).astype(x.dtype)

def rope_tables(n_tokens):
    rows = n_tokens // GRID_W
    row = jnp.repeat(jnp.arange(rows), GRID_W).astype(jnp.float32)
    col = jnp.tile(jnp.arange(GRID_W), rows).astype(jnp.float32)
    half = HEAD_DIM // 2
    inv = ROPE_THETA ** (-jnp.arange(0, half, 2, dtype=jnp.float32) / half)
    ang = jnp.concatenate([row[:, None] * inv, col[:, None] * inv], axis=-1)
    return jnp.cos(ang), jnp.sin(ang)

def apply_rope(x, cos, sin):
    xf = x.astype(jnp.float32).reshape(*x.shape[:-1], HEAD_DIM // 2, 2)
    x0, x1 = xf[..., 0], xf[..., 1]
    c = cos[None, :, None, :]
    s = sin[None, :, None, :]
    out = jnp.stack([x0 * c - x1 * s, x0 * s + x1 * c], axis=-1)
    return out.reshape(x.shape).astype(x.dtype)

def gqa(q, k, v):
    B, L = q.shape[:2]
    G = N_HEADS // N_KV_HEADS
    qg = q.reshape(B, L, N_KV_HEADS, G, HEAD_DIM)
    s = jnp.einsum('bqkgd,bskd->bkgqs', qg, k, preferred_element_type=jnp.float32) * (HEAD_DIM ** -0.5)
    p = jax.nn.softmax(s, axis=-1).astype(v.dtype)
    o = jnp.einsum('bkgqs,bskd->bqkgd', p, v)
    return o.reshape(B, L, ATTN_W)

def blocked_gqa(q, k, v):
    B, S = q.shape[:2]
    nb = S // Q_BLOCK
    qb = q.reshape(B, nb, Q_BLOCK, N_HEADS, HEAD_DIM).swapaxes(0, 1)
    o = lax.map(lambda qi: gqa(qi, k, v), qb)
    return o.swapaxes(0, 1).reshape(B, S, ATTN_W)

def conformer_conv(u, w_dw, b_dw, ln_g, ln_b):
    a, g = jnp.split(u, 2, axis=-1)
    y = a * jax.nn.sigmoid(g)
    y = lax.conv_general_dilated(
        y, w_dw[:, None, :].astype(y.dtype), window_strides=(1,),
        padding=[(CONV_K // 2, CONV_K // 2)],
        dimension_numbers=('NWC', 'WIO', 'NWC'), feature_group_count=CONV_W) + b_dw
    return jax.nn.silu(layernorm(y, ln_g, ln_b))

def split_heads(z, n):
    return z.reshape(*z.shape[:2], n, HEAD_DIM)

def mixer(h_lat, h_ctx, cos, sin, w_in, q_g, k_g, w_dw, b_dw, ln_g, ln_b, w_out, ctx_out):
    cuts = [ATTN_W, ATTN_W + KV_W, ATTN_W + 2 * KV_W]
    q, k, v, u = jnp.split(h_lat @ w_in, cuts, axis=-1)
    if ctx_out:
        qc, kc, vc, uc = jnp.split(h_ctx @ w_in, cuts, axis=-1)
    else:
        kc, vc = jnp.split(h_ctx @ w_in[:, ATTN_W:ATTN_W + 2 * KV_W], 2, axis=-1)
    q = apply_rope(rmsnorm(split_heads(q, N_HEADS), q_g), cos, sin)
    k = apply_rope(rmsnorm(split_heads(k, N_KV_HEADS), k_g), cos, sin)
    kc = rmsnorm(split_heads(kc, N_KV_HEADS), k_g)
    vc = split_heads(vc, N_KV_HEADS)
    k_all = jnp.concatenate([k, kc], axis=1)
    v_all = jnp.concatenate([split_heads(v, N_KV_HEADS), vc], axis=1)
    a_lat = blocked_gqa(q, k_all, v_all)
    c_lat = conformer_conv(u, w_dw, b_dw, ln_g, ln_b)
    o_lat = jnp.concatenate([a_lat, c_lat], axis=-1) @ w_out
    if not ctx_out:
        return o_lat, None
    qc = rmsnorm(split_heads(qc, N_HEADS), q_g)
    a_ctx = gqa(qc, kc, vc)
    c_ctx_out = conformer_conv(uc, w_dw, b_dw, ln_g, ln_b)
    o_ctx = jnp.concatenate([a_ctx, c_ctx_out], axis=-1) @ w_out
    return o_lat, o_ctx

def swiglu(h, w1, w3, w2):
    return (jax.nn.silu(h @ w1) * (h @ w3)) @ w2

def moe_swiglu(h, w_r, b_r, w1, w3, w2):
    B, L, D = h.shape
    hf = h.reshape(B * L, D)
    logits = (hf @ w_r).astype(jnp.float32) + b_r.astype(jnp.float32)
    top_v, top_i = lax.top_k(logits, TOP_K)
    gates = jax.nn.softmax(top_v, axis=-1)
    combine = jnp.sum(jax.nn.one_hot(top_i, N_EXPERTS, dtype=jnp.float32) * gates[..., None], axis=-2)
    combine = combine.astype(h.dtype)
    out = jnp.zeros_like(hf)
    for e in range(N_EXPERTS):
        out = out + combine[:, e:e + 1] * swiglu(hf, w1[e], w3[e], w2[e])
    return out.reshape(B, L, D)

def modulation(cvec, w_ada, b_ada):
    return jnp.split(jax.nn.silu(cvec) @ w_ada + b_ada, 6, axis=-1)

def setup_inputs(seed: int = 0) -> dict:
    key = jax.random.key(seed)
    ks = jax.random.split(key, 32)
    f32 = jnp.float32
    n_dense = (DEPTH + 1) // 2
    n_moe = DEPTH // 2

    def nrm(k, shape, scale):
        return jax.random.normal(k, shape, f32) * scale

    return dict(
        x=nrm(ks[0], (BATCH, SEQ, D_MODEL), 1.0),
        c=nrm(ks[1], (BATCH, D_MODEL), 1.0),
        ctx=nrm(ks[2], (BATCH, CTX_LEN, D_MODEL), 1.0),
        c_ctx=nrm(ks[3], (D_MODEL,), 1.0),
        w_ada=nrm(ks[4], (DEPTH, D_MODEL, 6 * D_MODEL), D_MODEL ** -0.5),
        b_ada=nrm(ks[5], (DEPTH, 6 * D_MODEL), 0.01),
        norm1_g=1.0 + nrm(ks[6], (DEPTH, D_MODEL), 0.01),
        w_in=nrm(ks[7], (DEPTH, D_MODEL, IN_W), D_MODEL ** -0.5),
        q_norm_g=1.0 + nrm(ks[8], (DEPTH, HEAD_DIM), 0.01),
        k_norm_g=1.0 + nrm(ks[9], (DEPTH, HEAD_DIM), 0.01),
        dw_w=nrm(ks[10], (DEPTH, CONV_K, CONV_W), CONV_K ** -0.5),
        dw_b=nrm(ks[11], (DEPTH, CONV_W), 0.01),
        conv_ln_g=1.0 + nrm(ks[12], (DEPTH, CONV_W), 0.01),
        conv_ln_b=nrm(ks[13], (DEPTH, CONV_W), 0.01),
        w_out=nrm(ks[14], (DEPTH, MIX_W, D_MODEL), MIX_W ** -0.5),
        norm2_g=1.0 + nrm(ks[15], (DEPTH, D_MODEL), 0.01),
        ffn_w1=nrm(ks[16], (n_dense, D_MODEL, D_FF), D_MODEL ** -0.5),
        ffn_w3=nrm(ks[17], (n_dense, D_MODEL, D_FF), D_MODEL ** -0.5),
        ffn_w2=nrm(ks[18], (n_dense, D_FF, D_MODEL), D_FF ** -0.5),
        router_w=nrm(ks[19], (n_moe, D_MODEL, N_EXPERTS), D_MODEL ** -0.5),
        router_b=nrm(ks[20], (n_moe, N_EXPERTS), 0.01),
        exp_w1=nrm(ks[21], (n_moe, N_EXPERTS, D_MODEL, D_FF), D_MODEL ** -0.5),
        exp_w3=nrm(ks[22], (n_moe, N_EXPERTS, D_MODEL, D_FF), D_MODEL ** -0.5),
        exp_w2=nrm(ks[23], (n_moe, N_EXPERTS, D_FF, D_MODEL), D_FF ** -0.5),
        final_g=1.0 + nrm(ks[24], (D_MODEL,), 0.01),
    )

def reference(x, c, ctx, c_ctx, w_ada, b_ada, norm1_g, w_in, q_norm_g, k_norm_g, dw_w, dw_b,
              conv_ln_g, conv_ln_b, w_out, norm2_g, ffn_w1, ffn_w3, ffn_w2, router_w, router_b,
              exp_w1, exp_w3, exp_w2, final_g):
    cos, sin = rope_tables(x.shape[1])
    xc = ctx
    for l in range(DEPTH):
        last = l == DEPTH - 1
        sh1, sc1, g1, sh2, sc2, g2 = [m[:, None, :] for m in modulation(c, w_ada[l], b_ada[l])]
        csh1, csc1, cg1, csh2, csc2, cg2 = modulation(c_ctx, w_ada[l], b_ada[l])
        h_lat = rmsnorm(x, norm1_g[l]) * (1.0 + sc1) + sh1
        h_ctx = rmsnorm(xc, norm1_g[l]) * (1.0 + csc1) + csh1
        o_lat, o_ctx = mixer(h_lat, h_ctx, cos, sin, w_in[l], q_norm_g[l], k_norm_g[l],
                             dw_w[l], dw_b[l], conv_ln_g[l], conv_ln_b[l], w_out[l], not last)
        x = x + g1 * o_lat
        h_lat = rmsnorm(x, norm2_g[l]) * (1.0 + sc2) + sh2
        if l % 2 == 0:
            i = l // 2
            f_lat = swiglu(h_lat, ffn_w1[i], ffn_w3[i], ffn_w2[i])
        else:
            i = l // 2
            f_lat = moe_swiglu(h_lat, router_w[i], router_b[i], exp_w1[i], exp_w3[i], exp_w2[i])
        if not last:
            xc = xc + cg1 * o_ctx
            h_ctx = rmsnorm(xc, norm2_g[l]) * (1.0 + csc2) + csh2
            if l % 2 == 0:
                f_ctx = swiglu(h_ctx, ffn_w1[i], ffn_w3[i], ffn_w2[i])
            else:
                f_ctx = moe_swiglu(h_ctx, router_w[i], router_b[i], exp_w1[i], exp_w3[i], exp_w2[i])
            xc = xc + cg2 * f_ctx
        x = x + g2 * f_lat
    return rmsnorm(x, final_g)


_drawn_inputs = setup_inputs


def setup_inputs(seed=0):
    import zlib

    import numpy as np

    out = dict(_drawn_inputs(seed))
    spreads = {}
    factors = {'norm1_g': 8.0,
     'q_norm_g': 8.0,
     'k_norm_g': 8.0,
     'dw_b': 8.0,
     'conv_ln_g': 4.259,
     'conv_ln_b': 5.171,
     'router_b': 30.343,
     'final_g': 32.361,
     'norm2_g': 3.202}
    for name, (base, spread) in spreads.items():
        noise = np.random.default_rng([zlib.crc32(name.encode()), seed]).standard_normal(out[name].shape)
        drawn = base * np.exp(spread * noise) if base else spread * noise
        out[name] = __import__('jax').numpy.asarray(drawn.astype(out[name].dtype))
    for name, factor in factors.items():
        out[name] = (out[name] * factor).astype(out[name].dtype)
    return out
```

```python
from contextlib import ExitStack

import concourse.bass as bass
from concourse import mybir

ALU = mybir.AluOpType
ACT = mybir.ActivationFunctionType
F32 = mybir.dt.float32
AX = mybir.AxisListType.X

P = 128
D = 1024
KT = D // P
S = 256
TT = 2 * S
HD = 64
NQ = 512
NC = 4
INW = 1792
TAPS = 31
PAD = TAPS // 2
FF = 2816
NF = FF // P
NE = 8
EPS = 1e-6
C = 96
ROUNDS = -(-S // C)
BIG = 1000.0
SLOTS = 5
SLOT = 2 * 3 * D
OFF = [s * SLOT for s in range(SLOTS)]
TAIL = OFF[4] + SLOT
RING = TAIL + 3 * D
MOE0 = 41

CONSTS = ["ident", "mean_d", "mean_head", "mean_conv", "rot", "halves", "before", "ones"]
COS = len(CONSTS) * P
SIN = COS + S
IOTA = SIN + S
REV = IOTA + 3 * C
NCONST = REV + NE


def tiles_in(k):
    return 3 if (MOE0 + k) % SLOTS == 4 else 2


FIRST = [sum(tiles_in(i) for i in range(k)) for k in range(11)]
assert FIRST[10] == NF


def backbone(nc, t, out):
    with ExitStack() as ctx:
        def sb(name, cols, rows=P):
            return ctx.enter_context(nc.sbuf_tensor(name, [rows, cols], F32))

        def sem(name):
            return ctx.enter_context(nc.semaphore(name))

        ring = sb("weight_ring", RING)
        xT = sb("xT", KT * TT)
        hT = sb("hT", KT * TT)
        scr = sb("scratch", 8192)
        con = sb("constants", NCONST)
        vec1 = sb("vec1", 120)
        vec2 = sb("vec2", 56)
        dwt = sb("conv_weights", 248)
        rows = scr[:, 0:4 * P]
        qk_g = sb("qk_gain", 4)
        mod = sb("modulation", 2 * 96)
        gain = sb("norm_gain", 4 * 16)
        silu_c = sb("silu_c", 16)
        rw = sb("router_w", KT * NE)
        rb = sb("router_b", NE)
        att = sb("softmax_stats", 4 * 32)
        rt = sb("router_state", 2 * 80)
        posm = sb("slot_of_token", 2 * 9)
        comb = sb("gate_of_token", 2 * 9)
        cur = sb("current_expert", 4)
        small = sb("mask_of_token", 2 * NE)
        eps = sb("eps", 1)
        most = ctx.enter_context(nc.sbuf_tensor("most_tokens_of_an_expert", [P, 1], mybir.dt.int32))
        bank = [ctx.enter_context(nc.psum_tensor(f"bank{i}", [P, 512], F32)) for i in range(8)]

        xv = xT[:, :].rearrange("p (c t) -> p c t", c=KT)
        hv = hT[:, :].rearrange("p (c t) -> p c t", c=KT)
        xtok = hT[:, :].rearrange("p (n d) -> p n d", n=4)

        def const(name):
            i = CONSTS.index(name) * P
            return con[:, i:i + P]

        ident = const("ident")
        cos, sin = con[:, COS:COS + S], con[:, SIN:SIN + S]

        qn = [scr[:, i * TT:(i + 1) * TT] for i in range(5)]
        kswap = scr[:, 2560:3072]
        vtok = scr[:, 3072:3584].rearrange("p (n d) -> p n d", n=4)
        ypad = scr[:, 3584:3584 + 8 * (S + 2 * PAD)].rearrange("p (c s t) -> p c s t", c=NC, s=2)
        o = 3584 + 8 * (S + 2 * PAD)
        tmpA = [scr[:, o:o + 512], scr[:, o + 512:o + 1024]]
        diag = [scr[:, o + 1024:o + 1152], scr[:, o + 1152:o + 1280]]
        rstd = scr[:, o + 1280:o + 1792]
        assert o + 1792 <= 8192
        acc = [ring[:, TAIL + i * 512:TAIL + (i + 1) * 512] for i in range(NC)]
        tmpB = [ring[:, TAIL + 2048 + i * 512:TAIL + 2560 + i * 512] for i in range(2)]
        aT = [scr[:, i * 512:(i + 1) * 512] for i in range(16)] + \
             [ring[:, TAIL + i * 512:TAIL + (i + 1) * 512] for i in range(6)]
        h2tok = scr[:, 0:2048].rearrange("p (n d) -> p n d", n=2)
        fT = scr[:, 2048:4096].rearrange("p (c t) -> p c t", c=KT)
        xg = scr[:, 4096:4096 + KT * C].rearrange("p (c t) -> p c t", c=KT)
        yT = scr[:, 5120:5120 + KT * C].rearrange("p (c t) -> p c t", c=KT)
        ytok = scr[0:C, 6144:7168]
        sel = scr[:, 7168:7168 + 2 * C].rearrange("p (n t) -> p n t", n=2)
        selg = scr[:, 7424:7424 + 2 * C].rearrange("p (n t) -> p n t", n=2)
        sgT = scr[0:C, 7680:7936]
        ae = [scr[:, 7936:7936 + C], scr[:, 8064:8064 + C]]
        frstd = scr[:, 4096:4096 + S]
        otok = xT[:, :].rearrange("p (n d) -> p n d", n=4)

        mods = [mod[:, l * 96:(l + 1) * 96].rearrange("p (m v) -> p m v", v=2) for l in range(2)]
        gains = [[gain[:, (2 * l + i) * 16:(2 * l + i + 1) * 16].rearrange("p (m v) -> p m v", v=2)
                  for i in range(2)] for l in range(2)]
        silu_cv = silu_c[:, :].rearrange("p (k v) -> p k v", v=2)

        names = ["mod_mm", "mod_ready", "gain_ready", "sq1", "st1", "root1", "root2", "qk_root", "ln_root", "scaled1", "h1_ready",
                 "qk_mm", "qk_sq", "qk_raw", "qk_stat", "qk_rstd", "qk_norm", "qk_rot", "roped",
                 "ks_mm", "ks_ready", "v_mm", "v_ready", "u_mm", "u_sig", "glu", "pad_zero",
                 "conv_step", "sc_mm", "nb_ready", "exp_done", "diag_ready", "pt_mm", "pt_ready",
                 "pv_mm", "o_ready", "mean_mm", "centred", "ln_sq", "var_mm", "ln_scaled", "mix_ready",
                 "wo_mm", "x1", "sq2", "st2", "scaled2", "h2_ready"]
        L = [{n: sem(f"{n}_{l}") for n in names} for l in range(2)]
        const_in, rows_in, x_in, vec_in = sem("const_in"), sem("rows_in"), sem("x_in"), sem("vec_in")
        vec_mm, vec_ready, xt_mm, xt_ready, silu_ready = (
            sem("vec_mm"), sem("vec_ready"), sem("xt_mm"), sem("xt_ready"), sem("silu_ready"))
        f_mm, f_silu, a_ready, y_mm, x2 = sem("f_mm"), sem("f_silu"), sem("a_ready"), sem("y_mm"), sem("x2")
        tok_mm, tok_ready, lg_mm, dm_ready, ed_ready, mask_ready, pos_mm, pos_ready = (
            sem(n) for n in ["tok_mm", "tok_ready", "lg_mm", "dm_ready", "ed_ready", "mask_ready",
                             "pos_mm", "pos_ready"])
        sel_ready, g_mm, xg_ready, eh_mm, e_silu, ea_ready, w2_mm = (
            sem(n) for n in ["sel_ready", "g_mm", "xg_ready", "eh_mm", "e_silu", "ea_ready", "w2_mm"])
        st_mm, sgt_ready, yT_ready, yt_mm, ytok_ready, sc_e, acc_done = (
            sem(n) for n in ["st_mm", "sgt_ready", "yT_ready", "yt_mm", "ytok_ready", "sc_e", "acc_done"])
        xf, sqf, stf, rootf, outn, ot_mm, ot_ready, stored = (
            sem(n) for n in ["xf", "sqf", "stf", "rootf", "outn", "ot_mm", "ot_ready", "stored"])
        filled = [sem(f"slot_filled_{s}") for s in range(SLOTS)]
        dve_chain = sem("dve_chain")
        cur_ready, most_ready = sem("cur_ready"), sem("most_ready")
        eps_ready = sem("eps_ready")

        def k_major(w, a, b):
            return w.rearrange("(k p) n -> p k n", p=P)[:, :, a:b]

        def slot(n, k, w, at=0):
            a = OFF[n % SLOTS] + at
            return ring[:, a:a + k * w].rearrange("p (k n) -> p k n", k=k)

        fills = []

        def fill(parts, free):
            n = len(fills)
            fills.append(([(slot(n, k, w, at), src) for k, w, at, src in parts], free))
            return n

        F = [{}, {}]
        for l in range(2):
            m = L[l]

            def ada(n):
                fill([(KT, 768, 0, k_major(t["w_ada"][l], 768 * n, 768 * (n + 1)))], (m["mod_mm"], n + 1))

            F[l]["ada"] = []
            for n in range(3):
                F[l]["ada"].append(len(fills))
                ada(n)
            F[l]["qkv"] = fill([(KT, 768, 0, k_major(t["w_in"][l], 0, 768))], (m["v_mm"], 1))
            F[l]["u"] = [fill([(KT, 256, 0, k_major(t["w_in"][l], 768 + 256 * i, 1024 + 256 * i)),
                               (KT, 256, KT * 256, k_major(t["w_in"][l], 1280 + 256 * i, 1536 + 256 * i))],
                              (m["u_mm"], 2 * i + 2)) for i in range(2)]
            for n in range(3, 8):
                F[l]["ada"].append(len(fills))
                ada(n)
            F[l]["wo"] = [fill([(KT, 512, 0, k_major(t["w_out"][l], 512 * i, 512 * i + 512))],
                               (m["wo_mm"], 4 * i + 4)) for i in range(2)]
            if l == 0:
                F[l]["w13"] = [fill([(KT, 256, 0, k_major(t["ffn_w1"][0], 256 * g, 256 * g + 256)),
                                     (KT, 256, KT * 256, k_major(t["ffn_w3"][0], 256 * g, 256 * g + 256))],
                                    (f_mm, 2 * g + 2)) for g in range(NF // 2)]
                F[l]["w2"] = [fill([(NF, 256, 0, k_major(t["ffn_w2"][0], 256 * g, 256 * g + 256))],
                                   (y_mm, 2 * g + 2)) for g in range(KT // 2)]
        assert len(fills) == MOE0
        level = [0] * SLOTS
        landed = []
        for n, (parts, _) in enumerate(fills):
            level[n % SLOTS] += 16 * len(parts)
            landed.append(level[n % SLOTS])

        def arrived(eng, n):
            eng.wait_ge(filled[n % SLOTS], landed[n])

        def units(l):
            u = [(c, hh, qt, 0, 0) for c in range(NC) for hh in range(2) for qt in range(2)]
            if l == 0:
                u += [(c, hh, qt, 2, 1) for c in range(NC) for hh in range(2) for qt in range(2)]
            return u

        segs = [[0, 1], [0]]

        def rounds(eng, body):
            body(0)
            eng.wait_ge(most_ready, 1)
            n = eng.value_load(most[0:1, 0:1], min_val=0, max_val=S)
            for r in range(1, ROUNDS):
                with eng.If(n > r * C):
                    body(r)

        block = ctx.enter_context(nc.Block())

        @block.sync
        def _(sp):
            sp.dma_start(rows[0:48, 0:P], t["b_ada"][0].rearrange("(a p) -> a p", p=P)).then_inc(rows_in, 16)
            sp.dma_start(rows[48:96, 0:P], t["b_ada"][1].rearrange("(a p) -> a p", p=P)).then_inc(rows_in, 16)
            sp.dma_start(rows[96:104, 0:P], t["c"].rearrange("b (a p) -> (b a) p", p=P)).then_inc(rows_in, 16)
            sp.dma_start(rows[104:112, 0:P], t["c_ctx"].rearrange("(a p) -> a p", p=P)).then_inc(rows_in, 16)
            sp.dma_start(rows[112:120, 0:P], t["final_g"].rearrange("(a p) -> a p", p=P)).then_inc(rows_in, 16)
            at = 0
            for name, n in [("norm1_g", 16), ("norm2_g", 16), ("dw_b", 8), ("conv_ln_g", 8), ("conv_ln_b", 8)]:
                sp.dma_start(rows[at:at + n, P:2 * P],
                             t[name].rearrange("l (a p) -> (l a) p", p=P)).then_inc(rows_in, 16)
                at += n
            for l in range(2):
                sp.dma_start(rows[0:TAPS * NC, (2 + l) * P:(3 + l) * P],
                             t["dw_w"][l].rearrange("k (a p) -> (k a) p", p=P)).then_inc(rows_in, 16)
            for n, (parts, free) in enumerate(fills):
                if n >= SLOTS:
                    sp.wait_ge(*fills[n - SLOTS][1])
                for dst, src in parts:
                    sp.dma_start(dst, src).then_inc(filled[n % SLOTS], 16)

            def expert_fill(k, e):
                s = (MOE0 + k) % SLOTS
                w = tiles_in(k) * P
                a, f = OFF[s], FIRST[k] * P
                for i, name in enumerate(["exp_w1", "exp_w3"]):
                    src = t[name][0, e].rearrange("(k p) n -> p k n", p=P)[:, :, f:f + w]
                    dst = ring[:, a + i * KT * w:a + (i + 1) * KT * w].rearrange("p (k n) -> p k n", k=KT)
                    sp.dma_start(dst, src).then_inc(filled[s], 16)
                src = t["exp_w2"][0, e][f:f + w, :].rearrange("(k p) n -> p k n", p=P)
                dst = ring[:, a + 2 * KT * w:a + 3 * KT * w].rearrange("p (k n) -> p k n", n=D)
                sp.dma_start(dst, src).then_inc(filled[s], 16)

            def expert_weights(r):
                base = NE * r
                for k in range(SLOTS):
                    if r == 0:
                        n = MOE0 + k - SLOTS
                        sp.wait_ge(*fills[n][1])
                        if (MOE0 + k) % SLOTS == 4:
                            sp.wait_ge(L[1]["mix_ready"], NC)
                    else:
                        sp.wait_ge(w2_mm, NF * (base - 1) + FIRST[k + SLOTS + 1])
                    expert_fill(k, 0)
                with sp.Fori(0, NE - 1) as e:
                    for k in range(SLOTS, 2 * SLOTS):
                        sp.wait_ge(w2_mm, NF * e + (NF * base + FIRST[k - SLOTS + 1]))
                        expert_fill(k, e)
                    for k in range(SLOTS):
                        sp.wait_ge(w2_mm, NF * e + (NF * base + FIRST[k + SLOTS + 1]))
                        expert_fill(k, e + 1)
                for k in range(SLOTS, 2 * SLOTS):
                    sp.wait_ge(w2_mm, NF * (base + NE - 1) + FIRST[k - SLOTS + 1])
                    expert_fill(k, NE - 1)

            rounds(sp, expert_weights)
            for n in range(2):
                sp.wait_ge(ot_ready, 2 * n + 2)
                sp.dma_start(out[0, n * P:(n + 1) * P, :], otok[:, 2 + n, :]).then_inc(stored, 16)
            sp.wait_ge(stored, 32)

        @block.tensor
        def _(pe):
            mm = pe.matmul
            pe.wait_ge(const_in, 16)
            pe.wait_ge(rows_in, 16 * 12)
            pe.transpose(bank[7][:, 0:120], rows[0:120, 0:P], ident[0:120, 0:120])
            pe.transpose(bank[7][:, 120:176], rows[0:56, P:2 * P], ident[0:56, 0:56])
            pe.transpose(bank[7][:, 176:300], rows[0:124, 2 * P:3 * P], ident[0:124, 0:124])
            pe.transpose(bank[7][:, 300:424], rows[0:124, 3 * P:4 * P], ident[0:124, 0:124]).then_inc(vec_mm, 1)
            pe.wait_ge(x_in, 32)
            for c in range(KT):
                if c >= 2:
                    pe.wait_ge(xt_ready, c - 1)
                for n in range(4):
                    i = pe.transpose(bank[c % 2][:, n * P:(n + 1) * P], xtok[:, n, c * P:(c + 1) * P], ident)
                i.then_inc(xt_mm, 1)

            def modulate(l, part):
                m = L[l]
                if l == 0 and part == 0:
                    pe.wait_ge(silu_ready, 1)
                for n in part:
                    arrived(pe, F[l]["ada"][n])
                    w = slot(F[l]["ada"][n], KT, 768)
                    for j in range(6):
                        col = 2 * (6 * n + j)
                        for k in range(KT):
                            i = mm(bank[6][:, col:col + 2], w[:, k, j * P:(j + 1) * P], silu_cv[:, k, :],
                                   start=(k == 0), stop=(k == KT - 1))
                    i.then_inc(m["mod_mm"], 1)

            def norm_stats(sq, st, T):
                for k in range(KT):
                    pe.wait_ge(sq, k + 1)
                    i = mm(bank[4][:, 0:T], const("mean_d"), hv[:, k, 0:T], start=(k == 0), stop=(k == KT - 1))
                i.then_inc(st, 1)

            for l in range(2):
                m = L[l]
                ns = len(segs[l])
                TQ = ns * S
                if l == 0:
                    pe.wait_ge(silu_ready, 2)
                modulate(l, range(3))
                if l == 1:
                    pe.wait_ge(x2, 2 * KT)
                norm_stats(m["sq1"], m["st1"], TT)
                pe.wait_ge(m["h1_ready"], 2 * KT)
                arrived(pe, F[l]["qkv"])
                w = slot(F[l]["qkv"], KT, 768)
                for i_ in range(7):
                    if i_ < 5:
                        j = i_
                        T = TQ if j < 4 else TT
                        if j >= 2:
                            pe.wait_ge(m["qk_sq"], j - 1)
                            pe.wait_ge(m["qk_raw"], j - 1)
                        for k in range(KT):
                            i = mm(bank[j % 2][:, 0:T], w[:, k, j * P:(j + 1) * P], hv[:, k, 0:T],
                                   start=(k == 0), stop=(k == KT - 1))
                        i.then_inc(m["qk_mm"], 1)
                    j = i_ - 1
                    if 0 <= j < 5:
                        T = TQ if j < 4 else TT
                        pe.wait_ge(m["qk_sq"], j + 1)
                        if j >= 2:
                            pe.wait_ge(m["qk_rstd"], j - 1)
                        mm(bank[2 + j % 2][:, 0:T], const("mean_head"), tmpA[j % 2][:, 0:T],
                           start=True, stop=True).then_inc(m["qk_stat"], 1)
                    j = i_ - 2
                    if 0 <= j < 5:
                        pe.wait_ge(m["qk_norm"], j + 1)
                        if j >= 2:
                            pe.wait_ge(m["roped"], j - 1)
                        mm(bank[4 + j % 2][:, 0:S], const("rot"), qn[j][:, 0:S],
                           start=True, stop=True).then_inc(m["qk_rot"], 1)
                for n in range(4):
                    for k in range(KT):
                        i = mm(bank[7][:, n * P:(n + 1) * P], hv[:, k, n * P:(n + 1) * P], w[:, k, 640:768],
                               start=(k == 0), stop=(k == KT - 1))
                i.then_inc(m["v_mm"], 1)
                for c in range(NC):
                    arrived(pe, F[l]["u"][c // 2])
                    w = slot(F[l]["u"][c // 2], 2 * KT, 256)
                    if c == 0:
                        pe.wait_ge(m["qk_raw"], 5)
                        pe.wait_ge(m["qk_sq"], 5)
                        pe.wait_ge(m["qk_rstd"], 5)
                    if c >= 2:
                        pe.wait_ge(m["glu"], c - 1)
                    for half in range(2):
                        for k in range(KT):
                            i = mm(bank[2 * half + c % 2][:, 0:TQ],
                                   w[:, half * KT + k, (c % 2) * P:(c % 2 + 1) * P], hv[:, k, 0:TQ],
                                   start=(k == 0), stop=(k == KT - 1))
                    i.then_inc(m["u_mm"], 1)
                pe.wait_ge(m["roped"], 5)
                mm(bank[5][:, :], const("halves"), qn[4], start=True, stop=True).then_inc(m["ks_mm"], 1)
                modulate(l, range(3, 8))
                U = units(l)
                pe.wait_ge(m["glu"], NC)
                pe.wait_ge(m["ks_ready"], 1)
                pe.wait_ge(m["v_ready"], 1)
                for st in range(len(U) + 2):
                    if st < len(U):
                        c, hh, qt, k0, sg = U[st]
                        if st >= 2:
                            pe.wait_ge(m["exp_done"], st - 1)
                        kv = c // 2
                        key = qn[4] if kv == hh else kswap
                        p0 = HD * hh
                        q0 = sg * S + qt * P
                        mm(bank[st % 2][:, 0:TT - k0 * P], qn[c][p0:p0 + HD, q0:q0 + P], key[p0:p0 + HD, k0 * P:TT],
                           start=True, stop=True).then_inc(m["sc_mm"], 1)
                    u = st - 1
                    if 0 <= u < len(U):
                        nk = 4 - U[u][3]
                        pe.wait_ge(m["diag_ready"], u + 1)
                        if u >= 2:
                            pe.wait_ge(m["pt_ready"], u - 1)
                        for kt in range(nk):
                            i = mm(bank[2 + u % 2][:, kt * P:(kt + 1) * P], tmpA[u % 2][:, kt * P:(kt + 1) * P],
                                   diag[u % 2], start=True, stop=True)
                        i.then_inc(m["pt_mm"], 1)
                    u = st - 2
                    if 0 <= u < len(U):
                        c, hh, qt, k0, sg = U[u]
                        kv = c // 2
                        nk = 4 - k0
                        pe.wait_ge(m["pt_ready"], u + 1)
                        ci = u // 4
                        if u % 4 == 0 and ci >= 2:
                            pe.wait_ge(m["o_ready"], ci - 1)
                        for kt in range(nk):
                            i = mm(bank[4 + ci % 2][HD * hh:HD * hh + HD, qt * P:(qt + 1) * P],
                                   vtok[:, k0 + kt, kv * HD:(kv + 1) * HD], tmpB[u % 2][:, kt * P:(kt + 1) * P],
                                   start=(kt == 0), stop=(kt == nk - 1))
                        i.then_inc(m["pv_mm"], 1)
                pe.wait_ge(m["conv_step"], NC * TAPS)
                for c in range(NC):
                    i = mm(bank[7][:, 0:TQ], const("mean_conv"), acc[c][:, 0:TQ], start=(c == 0), stop=(c == 3))
                i.then_inc(m["mean_mm"], 1)
                pe.wait_ge(m["mod_ready"], 2)
                for c in range(NC):
                    pe.wait_ge(m["ln_sq"], c + 1)
                    i = mm(bank[6][:, 0:TQ], const("mean_conv"), (tmpA + tmpB)[c][:, 0:TQ],
                           start=(c == 0), stop=(c == 3))
                i.then_inc(m["var_mm"], 1)
                pe.wait_ge(m["exp_done"], len(U))
                pe.wait_ge(m["pt_ready"], len(U))
                pe.wait_ge(m["o_ready"], len(U) // 4)
                pe.wait_ge(m["mix_ready"], NC)
                for j in range(KT):
                    arrived(pe, F[l]["wo"][j // 4])
                    w = slot(F[l]["wo"][j // 4], KT, 512)
                    if j >= 4:
                        pe.wait_ge(m["x1"], ns * (j - 3))
                    for k in range(KT):
                        i = mm(bank[j % 4][:, 0:TQ], w[:, k, (j % 4) * P:(j % 4 + 1) * P], hv[:, k, 0:TQ],
                               start=(k == 0), stop=(k == KT - 1))
                    i.then_inc(m["wo_mm"], 1)
                norm_stats(m["sq2"], m["st2"], TQ)
                pe.wait_ge(m["x1"], ns * KT)
                pe.wait_ge(m["h2_ready"], ns * KT)
                if l == 0:
                    for n in range(NF):
                        arrived(pe, F[0]["w13"][n // 2])
                        w = slot(F[0]["w13"][n // 2], 2 * KT, 256)
                        if n >= 2:
                            pe.wait_ge(a_ready, n - 1)
                        for half in range(2):
                            for k in range(KT):
                                i = mm(bank[2 * half + n % 2][:, :], w[:, half * KT + k, (n % 2) * P:(n % 2 + 1) * P],
                                       hv[:, k, :], start=(k == 0), stop=(k == KT - 1))
                        i.then_inc(f_mm, 1)
                    pe.wait_ge(a_ready, NF)
                    for d in range(KT):
                        arrived(pe, F[0]["w2"][d // 2])
                        w = slot(F[0]["w2"][d // 2], NF, 256)
                        if d >= 2:
                            pe.wait_ge(x2, 2 * (d - 1))
                        for n in range(NF):
                            i = mm(bank[4 + d % 2][:, :], w[:, n, (d % 2) * P:(d % 2 + 1) * P], aT[n],
                                   start=(n == 0), stop=(n == NF - 1))
                        i.then_inc(y_mm, 1)

            for b in range(4):
                for c in range(4):
                    k = (b % 2) * 4 + c
                    i = pe.transpose(bank[b][:, c * P:(c + 1) * P],
                                     hv[:, k, (b // 2) * P:(b // 2 + 1) * P], ident)
                i.then_inc(tok_mm, 1)
            pe.wait_ge(rows_in, 16 * 12)
            pe.wait_ge(vec_in, 16 * 10)
            for n in range(2):
                for k in range(KT):
                    i = mm(bank[4][:, n * NE:(n + 1) * NE], hv[:, k, n * P:(n + 1) * P],
                           rw[:, k * NE:(k + 1) * NE], start=(k == 0), stop=(k == KT - 1))
            i.then_inc(lg_mm, 1)
            pe.wait_ge(mask_ready, 1)
            mask = [small[:, 0:NE], small[:, NE:2 * NE]]
            mm(bank[5][:, 0:NE], const("before"), mask[0], start=True, stop=True)
            mm(bank[5][:, NE:2 * NE], const("before"), mask[1], start=True, stop=False)
            mm(bank[5][:, NE:2 * NE], const("ones"), mask[0], start=False, stop=True)
            mm(bank[5][:, 2 * NE:3 * NE], const("ones"), mask[0], start=True, stop=False)
            mm(bank[5][:, 2 * NE:3 * NE], const("ones"), mask[1], start=False, stop=True).then_inc(pos_mm, 1)
            pe.wait_ge(tok_ready, 4)
            pe.wait_ge(pos_ready, 1)

            def expert(e, base):
                def at(v, per):
                    return per * e + (per * base + v)

                pe.wait_ge(sel_ready, at(1, 1))
                pe.wait_ge(ytok_ready, at(1, 2))
                for half in range(2):
                    for c in range(4):
                        for n in range(2):
                            k = half * 4 + c
                            i = mm(bank[4 + half][:, c * C:(c + 1) * C], h2tok[:, n, k * P:(k + 1) * P],
                                   sel[:, n, :], start=(n == 0), stop=(n == 1))
                    i.then_inc(g_mm, 1)

                def second(n, k, j):
                    s = (MOE0 + k) % SLOTS
                    w = tiles_in(k)
                    a = OFF[s] + 2 * KT * w * P + j * D
                    pe.wait_ge(ea_ready, at(n + 3, NF))
                    if n == 0:
                        pe.wait_ge(yT_ready, at(1, 2))
                    for d in range(KT):
                        i = mm(bank[2 + d // 4][:, (d % 4) * C:(d % 4 + 1) * C], ring[:, a + d * P:a + (d + 1) * P],
                               ae[n % 2], start=(n == 0 and d % 4 == 0), stop=(n == NF - 1),
                               skip_group_check=True)
                    i.then_inc(w2_mm, 1)

                pe.wait_ge(xg_ready, at(2, 2))
                prev = None
                for k in range(2 * SLOTS):
                    s = (MOE0 + k) % SLOTS
                    w = tiles_in(k) * P
                    a = OFF[s]
                    pe.wait_ge(filled[s], at(level[s] + 48 * (k // SLOTS + 1), 96))
                    for j in range(tiles_in(k)):
                        n = FIRST[k] + j
                        pe.wait_ge(ea_ready, at(n + 1, NF))
                        for half in range(2):
                            for q in range(KT):
                                col = a + (half * KT + q) * w + j * P
                                i = mm(bank[n % 2][:, half * C:(half + 1) * C], ring[:, col:col + P], xg[:, q, :],
                                       start=(q == 0), stop=(q == KT - 1))
                        i.then_inc(eh_mm, 1)
                        if prev is not None:
                            second(*prev)
                        prev = (n, k, j)
                        if n == 6:
                            pe.wait_ge(acc_done, at(1, 4))
                            for q in range(2):
                                i = pe.transpose(bank[6][0:C, q * P:(q + 1) * P], selg[:, q, :], ident)
                            i.then_inc(st_mm, 1)
                second(*prev)
                for half in range(2):
                    pe.wait_ge(yT_ready, at(half + 2, 2))
                    for c in range(4):
                        i = pe.transpose(bank[4 + half][0:C, c * P:(c + 1) * P], yT[:, half * 4 + c, :], ident)
                    i.then_inc(yt_mm, 1)
                pe.wait_ge(sgt_ready, at(1, 1))
                for pr in range(4):
                    pe.wait_ge(ytok_ready, at(pr // 2 + 2, 2))
                    if pr >= 2:
                        pe.wait_ge(acc_done, at(pr, 4))
                    for c in range(2):
                        k = 2 * pr + c
                        i = mm(bank[6 + pr % 2][:, c * S:(c + 1) * S], ytok[:, k * P:(k + 1) * P], sgT,
                               start=True, stop=True)
                    i.then_inc(sc_e, 1)

            def experts(r):
                with pe.Fori(0, NE) as e:
                    expert(e, NE * r)

            rounds(pe, experts)

            for k in range(KT):
                pe.wait_ge(sqf, k + 1)
                i = mm(bank[4][:, 0:S], const("mean_d"), hv[:, k, 0:S], start=(k == 0), stop=(k == KT - 1))
            i.then_inc(stf, 1)
            pe.wait_ge(outn, KT)
            for b in range(4):
                for c in range(4):
                    k = (b % 2) * 4 + c
                    i = pe.transpose(bank[b][:, c * P:(c + 1) * P], hv[:, k, (b // 2) * P:(b // 2 + 1) * P], ident)
                i.then_inc(ot_mm, 1)

        @block.scalar
        def _(act):
            act.dma_start(con[:, :], t["constants"]).then_inc(const_in, 16)
            act.dma_start(xtok[:, 0:2, :], t["x"][0].rearrange("(n p) d -> p n d", p=P)).then_inc(x_in, 16)
            act.dma_start(xtok[:, 2:4, :], t["ctx"][0].rearrange("(n p) d -> p n d", p=P)).then_inc(x_in, 16)
            for l in range(2):
                for i, name in enumerate(["q_norm_g", "k_norm_g"]):
                    for h in range(2):
                        act.dma_start(qk_g[h * HD:(h + 1) * HD, 2 * l + i:2 * l + i + 1],
                                      t[name][l].rearrange("(p a) -> p a", a=1)).then_inc(vec_in, 16)
            act.dma_start(rw[:, :].rearrange("p (k e) -> p k e", k=KT),
                          t["router_w"][0].rearrange("(k p) e -> p k e", p=P)).then_inc(vec_in, 16)
            act.dma_start(rb[:, :], t["router_b"][0:1, :].partition_broadcast(P)
                          if False else t["router_b"][0:1, :].to_broadcast([P, NE])).then_inc(vec_in, 16)
            f = act.activation

            def root(dst, bank_, T, stat, n, done):
                act.wait_ge(stat, n)
                f(dst[:, 0:T], bank_[:, 0:T], ACT.Sqrt, bias=eps[:, 0:1]).then_inc(done, 1)

            act.wait_ge(eps_ready, 1)
            act.wait_ge(vec_ready, 1)
            for v in range(2):
                f(silu_cv[:, :, v], vec1[:, 96 + 8 * v:104 + 8 * v], ACT.Silu).then_inc(silu_ready, 1)
            for c in range(KT):
                act.wait_ge(xt_mm, c + 1)
                f(xv[:, c, :], bank[c % 2][:, :], ACT.Copy).then_inc(xt_ready, 1)

            def shift(m, l, which, done, ready):
                n = 0
                for c in range(KT):
                    for sg in ([0, 1] if which == 0 else segs[l]):
                        act.wait_ge(m[done], n + 1)
                        h = hv[:, c, sg * S:(sg + 1) * S]
                        f(h, h, ACT.Identity, bias=mods[l][:, 24 * which + c, sg:sg + 1]).then_inc(m[ready], 1)
                        n += 1

            for l in range(2):
                m = L[l]
                ns = len(segs[l])
                TQ = ns * S
                if l == 0:
                    act.wait_ge(xt_mm, KT)
                    act.wait_ge(xt_ready, KT)
                for c in range(KT):
                    if l == 1:
                        act.wait_ge(x2, 2 * c + 2)
                    f(hv[:, c, :], xv[:, c, :], ACT.Square).then_inc(m["sq1"], 1)
                root(rstd, bank[4], TT, m["st1"], 1, m["root1"])
                act.wait_ge(m["mod_ready"], 1)
                shift(m, l, 0, "scaled1", "h1_ready")
                for st in range(6):
                    j = st
                    if j < 5:
                        T = TQ if j < 4 else TT
                        act.wait_ge(m["qk_mm"], j + 1)
                        if j >= 2:
                            act.wait_ge(m["qk_stat"], j - 1)
                        f(tmpA[j % 2][:, 0:T], bank[j % 2][:, 0:T], ACT.Square).then_inc(m["qk_sq"], 1)
                    j = st - 1
                    if j >= 0:
                        if j == 0:
                            act.wait_ge(m["scaled1"], 2 * KT)
                        else:
                            act.wait_ge(m["qk_norm"], j)
                        root(rstd, bank[2 + j % 2], TQ if j < 4 else TT, m["qk_stat"], j + 1, m["qk_root"])
                act.wait_ge(m["v_mm"], 1)
                f(scr[:, 3072:3584], bank[7][:, :], ACT.Copy).then_inc(m["v_ready"], 1)
                act.wait_ge(m["qk_stat"], 5)
                for c in range(NC):
                    act.wait_ge(m["u_mm"], c + 1)
                    if c >= 2:
                        act.wait_ge(m["glu"], c - 1)
                    f(tmpA[c % 2][:, 0:TQ], bank[2 + c % 2][:, 0:TQ], ACT.Sigmoid).then_inc(m["u_sig"], 1)
                act.wait_ge(m["ks_mm"], 1)
                f(kswap, bank[5][:, :], ACT.Copy).then_inc(m["ks_ready"], 1)
                U = units(l)
                act.wait_ge(m["glu"], NC)
                act.wait_ge(m["roped"], 5)
                for st in range(len(U) + 2):
                    if st < len(U):
                        act.wait_ge(m["nb_ready"], st + 1)
                        if st >= 2:
                            act.wait_ge(m["pt_mm"], st - 1)
                        n = TT - U[st][3] * P
                        f(tmpA[st % 2][:, 0:n], bank[st % 2][:, 0:n], ACT.Exp, bias=att[:, 32 + st:33 + st],
                          scale=HD ** -0.5, accum_out=att[:, 64 + st:65 + st]).then_inc(m["exp_done"], 1)
                    u = st - 1
                    if 0 <= u < len(U):
                        n = TT - U[u][3] * P
                        act.wait_ge(m["pt_mm"], u + 1)
                        if u >= 2:
                            act.wait_ge(m["pv_mm"], u - 1)
                        f(tmpB[u % 2][:, 0:n], bank[2 + u % 2][:, 0:n], ACT.Copy).then_inc(m["pt_ready"], 1)
                    u = st - 2
                    if 0 <= u < len(U) and u % 4 == 3:
                        c, _, _, _, sg = U[u]
                        act.wait_ge(m["pv_mm"], u + 1)
                        f(hv[:, c, sg * S:(sg + 1) * S], bank[4 + (u // 4) % 2][:, 0:S],
                          ACT.Copy).then_inc(m["o_ready"], 1)
                act.wait_ge(m["pt_mm"], len(U))
                act.wait_ge(m["pv_mm"], len(U))
                for c in range(NC):
                    act.wait_ge(m["centred"], c + 1)
                    f((tmpA + tmpB)[c][:, 0:TQ], acc[c][:, 0:TQ], ACT.Square).then_inc(m["ln_sq"], 1)
                root(rstd, bank[6], TQ, m["var_mm"], 1, m["ln_root"])
                for c in range(NC):
                    act.wait_ge(m["ln_scaled"], c + 1)
                    f(hv[:, NC + c, 0:TQ], acc[c][:, 0:TQ], ACT.Silu, bias=vec2[:, 48 + 4 * l + c:49 + 4 * l + c],
                      scale=vec2[:, 40 + 4 * l + c:41 + 4 * l + c]).then_inc(m["mix_ready"], 1)
                act.wait_ge(m["wo_mm"], KT)
                for c in range(KT):
                    act.wait_ge(m["x1"], ns * (c + 1))
                    f(hv[:, c, 0:TQ], xv[:, c, 0:TQ], ACT.Square).then_inc(m["sq2"], 1)
                act.wait_ge(m["ln_scaled"], NC)
                root(rstd, bank[4], TQ, m["st2"], 1, m["root2"])
                shift(m, l, 1, "scaled2", "h2_ready")
                if l == 0:
                    for n in range(NF):
                        act.wait_ge(f_mm, n + 1)
                        f(aT[n], bank[n % 2][:, :], ACT.Silu).then_inc(f_silu, 1)

            for b in range(4):
                act.wait_ge(tok_mm, b + 1)
                f(scr[:, b * 512:(b + 1) * 512], bank[b][:, :], ACT.Copy).then_inc(tok_ready, 1)
            for n in range(2):
                act.wait_ge(dm_ready, n + 1)
                f(rt[:, 80 * n + 74:80 * n + 75], rt[:, 80 * n + 73:80 * n + 74], ACT.Exp).then_inc(ed_ready, 1)

            def expert(e, base):
                def at(v, per):
                    return per * e + (per * base + v)

                for half in range(2):
                    act.wait_ge(g_mm, at(half + 1, 2))
                    f(scr[:, 4096 + half * 4 * C:4096 + (half + 1) * 4 * C], bank[4 + half][:, 0:4 * C],
                      ACT.Copy).then_inc(xg_ready, 1)
                for n in range(NF):
                    act.wait_ge(eh_mm, at(n + 1, NF))
                    if n >= 2:
                        act.wait_ge(w2_mm, at(n - 1, NF))
                    f(ae[n % 2], bank[n % 2][:, 0:C], ACT.Silu).then_inc(e_silu, 1)
                    if n == 8:
                        act.wait_ge(st_mm, at(2, 1))
                        f(sgT, bank[6][0:C, 0:S], ACT.Copy).then_inc(sgt_ready, 1)
                act.wait_ge(w2_mm, at(NF, NF))
                for half in range(2):
                    f(scr[:, 5120 + half * 4 * C:5120 + (half + 1) * 4 * C], bank[2 + half][:, 0:4 * C],
                      ACT.Copy).then_inc(yT_ready, 1)
                for half in range(2):
                    act.wait_ge(yt_mm, at(half + 1, 2))
                    f(ytok[:, half * 512:(half + 1) * 512], bank[4 + half][0:C, :],
                      ACT.Copy).then_inc(ytok_ready, 1)

            def experts(r):
                with act.Fori(0, NE) as e:
                    expert(e, NE * r)

            rounds(act, experts)
            for c in range(KT):
                act.wait_ge(xf, c + 1)
                f(hv[:, c, 0:S], xv[:, c, 0:S], ACT.Square).then_inc(sqf, 1)
            root(frstd, bank[4], S, stf, 1, rootf)
            for b in range(4):
                act.wait_ge(ot_mm, b + 1)
                f(otok[:, 2 + b // 2, (b % 2) * 512:(b % 2 + 1) * 512], bank[b][:, :],
                  ACT.Copy).then_inc(ot_ready, 1)

        @block.vector
        def _(dve):
            chain = [0]

            def link(ins):
                chain[0] += 1
                ins.then_inc(dve_chain, 1)
                dve.wait_ge(dve_chain, chain[0])

            ts, tt, stt = dve.tensor_scalar, dve.tensor_tensor, dve.scalar_tensor_tensor
            dve.memset(eps[:, :], EPS).then_inc(eps_ready, 1)
            dve.wait_ge(vec_mm, 1)
            dve.tensor_copy(vec1[:, :], bank[7][:, 0:120])
            dve.tensor_copy(vec2[:, :], bank[7][:, 120:176])
            dve.tensor_copy(dwt[:, :], bank[7][:, 176:424]).then_inc(vec_ready, 1)
            dve.wait_ge(vec_ready, 1)

            def scale(m, l, which, src, done, T):
                link(dve.reciprocal(rstd[:, 0:T], rstd[:, 0:T]))
                for c in range(KT):
                    for sg in range(T // S):
                        x = xv[:, c, sg * S:(sg + 1) * S]
                        stt(out=hv[:, c, sg * S:(sg + 1) * S], in0=x, scalar=gains[l][which][:, c, sg:sg + 1],
                            in1=rstd[:, sg * S:(sg + 1) * S], op0=ALU.mult, op1=ALU.mult).then_inc(m[done], 1)

            def residual(ps, l, c, gate, sg, done):
                x = xv[:, c, sg * S:(sg + 1) * S]
                stt(out=x, in0=ps[:, sg * S:(sg + 1) * S], scalar=mods[l][:, gate + c, sg:sg + 1],
                    in1=x, op0=ALU.mult, op1=ALU.add).then_inc(done, 1)

            def modulation(l, part):
                m = L[l]
                dve.wait_ge(m["mod_mm"], 8 if part else 3)
                a, b = (18, 48) if part else (0, 18)
                bias = vec1[:, l * 48 + a:l * 48 + b].rearrange("p (m v) -> p m v", v=1).to_broadcast([P, b - a, 2])
                ps = bank[6][:, 2 * a:2 * b].rearrange("p (m v) -> p m v", v=2)
                link(tt(mods[l][:, a:b, :], ps, bias, ALU.add))
                g = vec2[:, 16 * part + 8 * l:16 * part + 8 * l + 8]
                g = g.rearrange("p (m v) -> p m v", v=1).to_broadcast([P, KT, 2])
                s0 = 32 if part else 8
                stt(out=gains[l][part], in0=mods[l][:, s0:s0 + 8, :], scalar=1.0, in1=g,
                    op0=ALU.add, op1=ALU.mult).then_inc(m["mod_ready"], 1)
                dve.wait_ge(m["mod_ready"], part + 1)

            for l in range(2):
                m = L[l]
                ns = len(segs[l])
                TQ = ns * S
                modulation(l, 0)
                dve.wait_ge(m["root1"], 1)
                if l == 0:
                    dve.wait_ge(xt_ready, KT)
                scale(m, l, 0, "x", "scaled1", TT)
                dve.memset(ypad[:, :, :, 0:PAD], 0.0)
                link(dve.memset(ypad[:, :, :, PAD + S:], 0.0))
                dve.wait_ge(vec_in, 16 * 10)
                for st in range(7):
                    if st < 5:
                        j = st
                        T = TQ if j < 4 else TT
                        dve.wait_ge(m["qk_sq"], j + 1)
                        g = qk_g[:, 2 * l + j // 4:2 * l + j // 4 + 1]
                        ts(qn[j][:, 0:T], bank[j % 2][:, 0:T], g, None, ALU.mult).then_inc(m["qk_raw"], 1)
                    j = st - 1
                    if 0 <= j < 5:
                        T = TQ if j < 4 else TT
                        dve.wait_ge(m["qk_root"], j + 1)
                        dve.reciprocal(rstd[:, 0:T], rstd[:, 0:T]).then_inc(m["qk_rstd"], 1)
                        dve.wait_ge(m["qk_rstd"], j + 1)
                        dve.wait_ge(m["qk_raw"], j + 1)
                        tt(qn[j][:, 0:T], qn[j][:, 0:T], rstd[:, 0:T], ALU.mult).then_inc(m["qk_norm"], 1)
                    j = st - 2
                    if 0 <= j < 5:
                        dve.wait_ge(m["qk_norm"], j + 1)
                        if j >= 2:
                            dve.wait_ge(m["roped"], j - 1)
                        tt(tmpB[j % 2][:, 0:S], qn[j][:, 0:S], cos, ALU.mult)
                        dve.wait_ge(m["qk_rot"], j + 1)
                        link(tt(tmpB[j % 2][:, S:TT], bank[4 + j % 2][:, 0:S], sin, ALU.mult))
                        tt(qn[j][:, 0:S], tmpB[j % 2][:, 0:S], tmpB[j % 2][:, S:TT], ALU.add).then_inc(m["roped"], 1)
                for c in range(NC):
                    dve.wait_ge(m["u_sig"], c + 1)
                    a = bank[c % 2][:, 0:TQ].rearrange("p (s t) -> p s t", s=ns)
                    b = tmpA[c % 2][:, 0:TQ].rearrange("p (s t) -> p s t", s=ns)
                    tt(ypad[:, c, 0:ns, PAD:PAD + S], a, b, ALU.mult).then_inc(m["glu"], 1)

                def conv():
                    n = 0
                    for pair in range(2):
                        for k in range(TAPS):
                            for c in (2 * pair, 2 * pair + 1):
                                src = ypad[:, c, 0:ns, k:k + S]
                                dst = acc[c][:, 0:TQ].rearrange("p (s t) -> p s t", s=ns)
                                wk = dwt[:, 124 * l + 4 * k + c:124 * l + 4 * k + c + 1]
                                if k == 0:
                                    dve.wait_ge(m["glu"], c + 1)
                                    i = ts(dst, src, wk, vec2[:, 32 + 4 * l + c:33 + 4 * l + c], ALU.mult, ALU.add)
                                else:
                                    dve.wait_ge(m["conv_step"], n - 1)
                                    i = stt(out=dst, in0=src, scalar=wk, in1=dst, op0=ALU.mult, op1=ALU.add)
                                i.then_inc(m["conv_step"], 1)
                                n += 1
                                yield
                taps = conv()
                modulation_done = False
                U = units(l)
                per = -(-NC * TAPS // len(U))
                for st in range(len(U)):
                    n = TT - U[st][3] * P
                    dve.wait_ge(m["sc_mm"], st + 1)
                    link(dve.reduce_max(att[:, st:st + 1], bank[st % 2][:, 0:n], AX))
                    ts(att[:, 32 + st:33 + st], att[:, st:st + 1], -HD ** -0.5, None,
                       ALU.mult).then_inc(m["nb_ready"], 1)
                    for _ in range(per):
                        next(taps, None)
                    dve.wait_ge(m["exp_done"], st + 1)
                    link(dve.reciprocal(att[:, 96 + st:97 + st], att[:, 64 + st:65 + st]))
                    if st >= 2:
                        dve.wait_ge(m["pt_mm"], st - 1)
                    ts(diag[st % 2], ident, att[:, 96 + st:97 + st], None, ALU.mult).then_inc(m["diag_ready"], 1)
                for _ in taps:
                    pass
                modulation(l, 1)
                dve.wait_ge(m["mean_mm"], 1)
                dve.wait_ge(m["conv_step"], NC * TAPS)
                for c in range(NC):
                    tt(acc[c][:, 0:TQ], acc[c][:, 0:TQ], bank[7][:, 0:TQ], ALU.subtract).then_inc(m["centred"], 1)
                dve.wait_ge(m["centred"], NC)
                dve.wait_ge(m["ln_root"], 1)
                link(dve.reciprocal(rstd[:, 0:TQ], rstd[:, 0:TQ]))
                for c in range(NC):
                    tt(acc[c][:, 0:TQ], acc[c][:, 0:TQ], rstd[:, 0:TQ], ALU.mult).then_inc(m["ln_scaled"], 1)
                for c in range(KT):
                    dve.wait_ge(m["wo_mm"], c + 1)
                    for sg in segs[l]:
                        residual(bank[c % 4], l, c, 16, sg, m["x1"])
                dve.wait_ge(m["x1"], ns * KT)
                dve.wait_ge(m["root2"], 1)
                scale(m, l, 1, "x1", "scaled2", TQ)
                if l == 0:
                    for n in range(NF):
                        dve.wait_ge(f_silu, n + 1)
                        tt(aT[n], aT[n], bank[2 + n % 2][:, :], ALU.mult).then_inc(a_ready, 1)
                    for c in range(KT):
                        dve.wait_ge(y_mm, c + 1)
                        for sg in (0, 1):
                            residual(bank[4 + c % 2], 0, c, 40, sg, x2)
                    dve.wait_ge(x2, 2 * KT)

            dve.wait_ge(tok_mm, 4)
            dve.memset(scr[:, 2048:4096], 0.0)
            dve.memset(posm[:, :], BIG)
            link(dve.memset(comb[:, :], 0.0))
            pv = posm[:, :].rearrange("p (e n) -> p e n", n=2)
            cv = comb[:, :].rearrange("p (e n) -> p e n", n=2)
            rev = con[:, REV:REV + NE]
            dve.wait_ge(lg_mm, 1)
            for n in range(2):
                b = 80 * n
                lg, r1, s1, lg2, r2, s2, t1 = (rt[:, b + 8 * i:b + 8 * i + 8] for i in range(7))
                m1, q1, m2, q2, dm, ed, den, g1, g2 = (rt[:, b + i:b + i + 1] for i in (64, 65, 66, 67, 73, 74, 75, 76, 77))
                link(tt(lg, bank[4][:, n * NE:(n + 1) * NE], rb[:, :], ALU.add))
                link(dve.reduce_max(m1, lg, AX))
                link(stt(out=r1, in0=lg, scalar=m1, in1=rev, op0=ALU.is_equal, op1=ALU.mult))
                link(dve.reduce_max(q1, r1, AX))
                link(ts(s1, r1, q1, None, ALU.is_equal))
                link(stt(out=lg2, in0=s1, scalar=-3e38, in1=lg, op0=ALU.mult, op1=ALU.add))
                link(dve.reduce_max(m2, lg2, AX))
                link(stt(out=r2, in0=lg2, scalar=m2, in1=rev, op0=ALU.is_equal, op1=ALU.mult))
                link(dve.reduce_max(q2, r2, AX))
                link(ts(s2, r2, q2, None, ALU.is_equal))
                tt(dm, m2, m1, ALU.subtract).then_inc(dm_ready, 1)
                i = tt(small[:, n * NE:(n + 1) * NE], s1, s2, ALU.add)
                if n == 1:
                    i.then_inc(mask_ready, 1)
                dve.wait_ge(ed_ready, n + 1)
                link(ts(den, ed, 1.0, None, ALU.add))
                link(dve.reciprocal(g1, den))
                link(tt(g2, ed, g1, ALU.mult))
                link(ts(t1, s1, g1, None, ALU.mult))
                link(stt(out=cv[:, 0:NE, n], in0=s2, scalar=g2, in1=t1, op0=ALU.mult, op1=ALU.add))
            dve.wait_ge(mask_ready, 1)
            dve.wait_ge(pos_mm, 1)
            link(dve.reduce_max(rt[:, 78:79], bank[5][:, 2 * NE:3 * NE], AX))
            dve.tensor_copy(most[:, :], rt[:, 78:79]).then_inc(most_ready, 1)
            for n in range(2):
                far = rt[:, 80 * n:80 * n + 8]
                link(ts(far, small[:, n * NE:(n + 1) * NE], -BIG, BIG, ALU.mult, ALU.add))
                i = tt(pv[:, 0:NE, n], bank[5][:, n * NE:(n + 1) * NE], far, ALU.add)
                if n == 0:
                    link(i)
            i.then_inc(pos_ready, 1)
            dve.wait_ge(pos_ready, 1)
            link(dve.memset(cur[:, :], 0.0))
            dve.sem_inc(ea_ready, 2)
            for ahead in (ytok_ready, yT_ready, acc_done, st_mm):
                dve.sem_inc(ahead, 1)

            def select(e, r, step):
                dve.tensor_copy(cur[:, 0:2], pv[:, bass.ds(e, 1), :].rearrange("p a n -> p (a n)")
                                ).then_inc(cur_ready, 1)
                dve.tensor_copy(cur[:, 2:4], cv[:, bass.ds(e, 1), :].rearrange("p a n -> p (a n)")
                                ).then_inc(cur_ready, 1)
                dve.wait_ge(cur_ready, step)
                iota = con[:, IOTA + r * C:IOTA + (r + 1) * C]
                for n in range(2):
                    ts(sel[:, n, :], iota, cur[:, n:n + 1], None, ALU.is_equal)
                    i = ts(selg[:, n, :], iota, cur[:, n:n + 1], cur[:, 2 + n:3 + n], ALU.is_equal, ALU.mult)
                i.then_inc(sel_ready, 1)

            def expert(e, r, base):
                def at(v, per):
                    return per * e + (per * base + v)

                for n in range(NF):
                    dve.wait_ge(e_silu, at(n + 1, NF))
                    tt(ae[n % 2], ae[n % 2], bank[n % 2][:, C:2 * C], ALU.mult).then_inc(ea_ready, 1)
                for pr in range(4):
                    dve.wait_ge(sc_e, at(pr + 1, 4))
                    dst = fT[:, 2 * pr:2 * pr + 2, :]
                    tt(dst, dst, bank[6 + pr % 2][:, :].rearrange("p (c t) -> p c t", c=2),
                       ALU.add).then_inc(acc_done, 1)

            def experts(r):
                base = NE * r
                with dve.Fori(0, NE) as e:
                    dve.wait_ge(st_mm, e + (base + 1))
                    select(e, r, 2 * e + (2 * base + 2))
                    expert(e, r, base)
                dve.wait_ge(acc_done, 4 * NE * (r + 1) + 1)

            rounds(dve, experts)
            for c in range(KT):
                x = xv[:, c, 0:S]
                stt(out=x, in0=fT[:, c, :], scalar=mods[1][:, 40 + c, 0:1], in1=x,
                    op0=ALU.mult, op1=ALU.add).then_inc(xf, 1)
            dve.wait_ge(xf, KT)
            dve.wait_ge(rootf, 1)
            link(dve.reciprocal(frstd, frstd))
            for c in range(KT):
                stt(out=hv[:, c, 0:S], in0=xv[:, c, 0:S], scalar=vec1[:, 112 + c:113 + c], in1=frstd,
                    op0=ALU.mult, op1=ALU.mult).then_inc(outn, 1)


def tables():
    import numpy as np
    i = np.arange(P)
    m = {
        "ident": np.eye(P),
        "mean_d": np.full((P, P), 1 / D),
        "mean_head": (i[:, None] // HD == i[None, :] // HD) / HD,
        "mean_conv": np.full((P, P), 1 / 512),
        "rot": np.where((i[:, None] ^ 1) == i[None, :], np.where(i[None, :] % 2 == 0, -1.0, 1.0), 0.0),
        "halves": (i[:, None] + HD) % P == i[None, :],
        "before": i[:, None] < i[None, :],
        "ones": np.ones((P, P)),
    }
    tok = np.arange(S)
    inv = (np.float32(10000.0) ** (-np.arange(0, 32, 2, dtype=np.float32) / np.float32(32))).astype(np.float32)
    ang = np.concatenate([(tok // 64).astype(np.float32)[:, None] * inv,
                          (tok % 64).astype(np.float32)[:, None] * inv], axis=-1)
    pair = (i % HD) // 2
    cols = [np.asarray(m[n], np.float32) for n in CONSTS]
    cols += [np.cos(ang).T[pair].astype(np.float32), np.sin(ang).T[pair].astype(np.float32)]
    cols += [np.broadcast_to(np.arange(3 * C, dtype=np.float32), (P, 3 * C)),
             np.broadcast_to(np.arange(NE, 0, -1, dtype=np.float32), (P, NE))]
    return np.ascontiguousarray(np.concatenate(cols, axis=1), dtype=np.float32)


_INS = ["x", "c", "ctx", "c_ctx", "w_ada", "b_ada", "norm1_g", "w_in", "q_norm_g", "k_norm_g", "dw_w", "dw_b",
        "conv_ln_g", "conv_ln_b", "w_out", "norm2_g", "ffn_w1", "ffn_w3", "ffn_w2", "router_w", "router_b",
        "exp_w1", "exp_w3", "exp_w2", "final_g"]


def kernel(**inputs):
    import numpy as np
    import concourse.bacc as bacc
    from concourse.bass_utils import run_bass_kernel_spmd as run

    nc = bacc.Bacc("TRN2", target_bir_lowering=False, num_devices=1)
    arrays, t = {}, {}
    host = {n: np.ascontiguousarray(inputs[n]) for n in _INS}
    host["constants"] = tables()
    for name, a in host.items():
        arrays[f"in_{name}"] = a
        t[name] = nc.dram_tensor(f"in_{name}", a.shape, F32, kind="ExternalInput").ap()
    out = nc.dram_tensor("out", [1, S, D], F32, kind="ExternalOutput").ap()
    backbone(nc, t, out)
    r = run(nc, [arrays], core_ids=[0])
    return r.results[0]["out"]
```

```python
from contextlib import ExitStack

import concourse.bass as bass
from concourse import mybir

ALU = mybir.AluOpType
ACT = mybir.ActivationFunctionType
F32 = mybir.dt.float32
F32R = mybir.dt.float32r
AX = mybir.AxisListType.X

P = 128
D = 1024
KT = D // P
S = 256
TT = 2 * S
HD = 64
NQ = 512
NC = 4
INW = 1792
TAPS = 31
PAD = TAPS // 2
FF = 2816
NF = FF // P
NE = 8
EPS = 1e-6
C = 96
ROUNDS = -(-S // C)
BIG = 1000.0
SLOTS = 5
SLOT = 2 * 3 * D
OFF = [s * SLOT for s in range(SLOTS)]
TAIL = OFF[4] + SLOT
RING = TAIL + 3 * D
MOE0 = 56
STAGE = SLOTS - 1

CONSTS = ["ident", "mean_d", "mean_head", "mean_conv", "rot", "halves", "before", "ones"]
COS = len(CONSTS) * P
SIN = COS + S
IOTA = SIN + S
REV = IOTA + ROUNDS * C
NCONST = REV + NE


def expert_slot(k):
    return (MOE0 + 1 + k) % SLOTS


def tiles_in(k):
    return 3 if expert_slot(k) == SLOTS - 1 else 2


FIRST = [sum(tiles_in(i) for i in range(k)) for k in range(11)]
assert FIRST[10] == NF


def backbone(nc, t, out):
    with ExitStack() as ctx:
        def sb(name, cols, rows=P):
            return ctx.enter_context(nc.sbuf_tensor(name, [rows, cols], F32))

        def sem(name):
            return ctx.enter_context(nc.semaphore(name))

        def view(name, cols, base, at):
            return nc.alloc_sbuf_tensor_at(name, [P, cols], F32R, offset=base + 4 * at)

        ring = sb("weight_ring", RING)
        ring_base = nc.sbuf_base - 4 * RING
        slot_r = [view(f"slot_halves_{i}", SLOT, ring_base, OFF[i]) for i in range(SLOTS)]
        tail_r = view("tail_halves", RING - TAIL, ring_base, TAIL)
        xT = sb("xT", KT * TT)
        hT_base = nc.sbuf_base
        hT = sb("hT", KT * TT)
        hT_r = view("hT_halves", KT * TT, hT_base, 0)
        scr_base = nc.sbuf_base
        scr = sb("scratch", 8192)
        scr_r = view("scratch_halves", 8192, scr_base, 0)
        con = sb("constants", NCONST)
        vec1 = sb("vec1", 120)
        vec2 = sb("vec2", 56)
        dwt = sb("conv_weights", 248)
        rows = scr[:, 0:4 * P]
        qk_g = sb("qk_gain", 4)
        mod = sb("modulation", 2 * 96)
        gain = sb("norm_gain", 4 * 16)
        silu_c = sb("silu_c", 2 * KT + 32)
        rw = sb("router_w", KT * NE)
        rb = sb("router_b", NE)
        att = sb("softmax_stats", 4 * 32)
        rt = sb("router_state", 2 * 80)
        posm = sb("slot_of_token", 2 * 9)
        comb = sb("gate_of_token", 2 * 9)
        cur = sb("current_expert", 4)
        small = sb("mask_of_token", 2 * NE)
        eps = sb("eps", 1)
        most = ctx.enter_context(nc.sbuf_tensor("most_tokens_of_an_expert", [P, 1], mybir.dt.int32))
        bank = [ctx.enter_context(nc.psum_tensor(f"bank{i}", [P, 512], F32)) for i in range(8)]

        xv = xT[:, :].rearrange("p (c t) -> p c t", c=KT)
        hv = hT[:, :].rearrange("p (c t) -> p c t", c=KT)
        xtok = hT[:, :].rearrange("p (n d) -> p n d", n=4)

        def const(name):
            i = CONSTS.index(name) * P
            return con[:, i:i + P]

        ident = const("ident")
        cos, sin = con[:, COS:COS + S], con[:, SIN:SIN + S]

        qn = [scr[:, i * TT:(i + 1) * TT] for i in range(5)]
        kswap = scr[:, 2560:3072]
        vtok = scr[:, 3072:3584].rearrange("p (n d) -> p n d", n=4)
        ypad = scr[:, 3584:3584 + 8 * (S + 2 * PAD)].rearrange("p (c s t) -> p c s t", c=NC, s=2)
        o = 3584 + 8 * (S + 2 * PAD)
        tmpA = [scr[:, o:o + 512], scr[:, o + 512:o + 1024]]
        diag = [scr[:, o + 1024:o + 1152], scr[:, o + 1152:o + 1280]]
        rstd = scr[:, o + 1280:o + 1792]
        assert o + 1792 + 4 * P <= 8192
        acc = [ring[:, TAIL + i * 512:TAIL + (i + 1) * 512] for i in range(NC)]
        tmpB = [ring[:, TAIL + 2048 + i * 512:TAIL + 2560 + i * 512] for i in range(2)]
        aT = [scr[:, i * 512:(i + 1) * 512] for i in range(16)] + \
             [ring[:, TAIL + i * 512:TAIL + (i + 1) * 512] for i in range(6)]
        h2tok = scr[:, 0:2048].rearrange("p (n d) -> p n d", n=2)
        fT = scr[:, 2048:4096].rearrange("p (c t) -> p c t", c=KT)
        xg = scr[:, 4096:4096 + KT * C].rearrange("p (c t) -> p c t", c=KT)
        ytok = scr[0:C, 6144:7168]
        sel = scr[:, 7168:7168 + 2 * C].rearrange("p (n t) -> p n t", n=2)
        selg = scr[:, 7424:7424 + 2 * C].rearrange("p (n t) -> p n t", n=2)
        sgT = scr[0:C, 7680:7936]
        ae = [scr[:, 7936:7936 + C], scr[:, 8064:8064 + C]]
        w2_parts = hT_r
        w2_hi = [w2_parts[:, i * D:(i + 1) * D] for i in range(2)]
        w2_lo = [w2_parts[:, (2 + i) * D:(3 + i) * D] for i in range(2)]
        ae_parts = scr_r[:, 5120:5120 + 4 * P]
        ae_hi = [ae_parts[:, i * P:i * P + C] for i in range(2)]
        ae_lo = [ae_parts[:, (2 + i) * P:(2 + i) * P + C] for i in range(2)]

        def w2_row(n):
            k = max(i for i in range(10) if FIRST[i] <= n)
            a = OFF[expert_slot(k)] + 2 * KT * tiles_in(k) * P + (n - FIRST[k]) * D
            return ring[:, a:a + D]

        frstd = scr[:, 4096:4096 + S]
        otok = xT[:, :].rearrange("p (n d) -> p n d", n=4)

        mods = [mod[:, l * 96:(l + 1) * 96].rearrange("p (m v) -> p m v", v=2) for l in range(2)]
        gains = [[gain[:, (2 * l + i) * 16:(2 * l + i + 1) * 16].rearrange("p (m v) -> p m v", v=2)
                  for i in range(2)] for l in range(2)]
        silu_cv = silu_c[:, 0:2 * KT].rearrange("p (k v) -> p k v", v=2)
        mrow = [acc[0], acc[1]]
        cdiag = [scr[:, o + 1792 + i * P:o + 1792 + (i + 1) * P] for i in range(4)]

        names = ["mod_mm", "mod_row", "mod_t", "mod_done", "cd_ready", "cd_mm", "conv3", "sq1", "st1", "root",
                 "scaled1", "h1_ready",
                 "qk_mm", "qk_sq", "qk_raw", "qk_stat", "qk_rstd", "qk_norm", "qk_rot", "roped",
                 "ks_mm", "ks_ready", "v_mm", "v_ready", "u_mm", "u_sig", "glu",
                 "conv_step", "sc_mm", "nb_ready", "exp_done", "diag_ready", "pt_mm", "pt_ready",
                 "pv_mm", "o_ready", "mean_mm", "centred", "ln_sq", "var_mm", "ln_scaled", "mix_ready",
                 "wo_mm", "x1", "sq2", "st2", "scaled2", "h2_ready"]
        L = [{n: sem(f"{n}_{l}") for n in names} for l in range(2)]
        const_in, rows_in, x_in, vec_in = sem("const_in"), sem("rows_in"), sem("x_in"), sem("vec_in")
        vec_mm, vec_ready, xt_mm, xt_ready, silu_ready = (
            sem("vec_mm"), sem("vec_ready"), sem("xt_mm"), sem("xt_ready"), sem("silu_ready"))
        f_mm, f_silu, a_ready, y_mm, x2 = sem("f_mm"), sem("f_silu"), sem("a_ready"), sem("y_mm"), sem("x2")
        hi_ready, lo_ready, y_part = sem("hi_ready"), sem("lo_ready"), sem("y_part")
        tok_mm, tok_ready, lg_mm, dm_ready, ed_ready, mask_ready, pos_mm, pos_ready = (
            sem(n) for n in ["tok_mm", "tok_ready", "lg_mm", "dm_ready", "ed_ready", "mask_ready",
                             "pos_mm", "pos_ready"])
        sel_ready, g_mm, xg_ready, eh_mm, e_silu, ea_ready, w2_mm = (
            sem(n) for n in ["sel_ready", "g_mm", "xg_ready", "eh_mm", "e_silu", "ea_ready", "w2_mm"])
        st_mm, sgt_ready, sgt_zero, ytok_ready, sc_e, acc_done = (
            sem(n) for n in ["st_mm", "sgt_ready", "sgt_zero", "ytok_ready", "sc_e", "acc_done"])
        xf, sqf, stf, rootf, outn, ot_mm, ot_ready, stored = (
            sem(n) for n in ["xf", "sqf", "stf", "rootf", "outn", "ot_mm", "ot_ready", "stored"])
        filled = [sem(f"slot_filled_{s}") for s in range(SLOTS)]
        dve_chain = sem("dve_chain")
        w2hi_ready, ahi_ready, prod = sem("w2hi_ready"), sem("ahi_ready"), sem("prod")
        cur_ready, most_ready = sem("cur_ready"), sem("most_ready")
        eps_ready = sem("eps_ready")

        def k_major(w, a, b):
            return w.rearrange("(k p) n -> p k n", p=P)[:, :, a:b]

        fills, slot_of = [], []

        def slot(n, k, w, at=0, halves=False):
            s = slot_of[n]
            a = at if halves else OFF[s] + at
            return (slot_r[s] if halves else ring)[:, a:a + k * w].rearrange("p (k n) -> p k n", k=k)

        def fill(parts, free, s):
            n = len(fills)
            slot_of.append(s)
            fills.append(([(slot(n, k, w, at), src) for k, w, at, src in parts], free))
            return n

        F = [{}, {}]
        for l in range(2):
            m = L[l]
            first = len(fills)

            def turn():
                return (len(fills) - first) % SLOTS

            def ada(n):
                fill([(KT, 512, 0, k_major(t["w_ada"][l], 512 * n, 512 * (n + 1)))], (m["mod_mm"], n + 1), turn())

            F[l]["ada"] = []
            for n in range(4):
                F[l]["ada"].append(len(fills))
                ada(n)
            F[l]["qkv"] = fill([(KT, 768, 0, k_major(t["w_in"][l], 0, 768))], (m["v_mm"], 1), turn())
            F[l]["u"] = [fill([(KT, 256, 0, k_major(t["w_in"][l], 768 + 256 * i, 1024 + 256 * i)),
                               (KT, 256, KT * 256, k_major(t["w_in"][l], 1280 + 256 * i, 1536 + 256 * i))],
                              (m["u_mm"], 2 * i + 2), turn()) for i in range(2)]
            for n in range(4, 12):
                F[l]["ada"].append(len(fills))
                ada(n)
            F[l]["wo"] = [fill([(KT, 512, 0, k_major(t["w_out"][l], 512 * i, 512 * i + 512))],
                               (m["wo_mm"], 4 * i + 4), turn()) for i in range(2)]
            if l == 0:
                F[l]["w13"] = [fill([(KT, 256, 0, k_major(t["ffn_w1"][0], 256 * g, 256 * g + 256)),
                                     (KT, 256, KT * 256, k_major(t["ffn_w3"][0], 256 * g, 256 * g + 256))],
                                    (f_mm, 4 * g + 4), (g + 2) % STAGE) for g in range(NF // 2)]
                F[l]["w2"] = [fill([(2, D, 0, t["ffn_w2"][0][256 * g:256 * g + 256, :]
                                     .rearrange("(k p) n -> p k n", p=P))],
                                   (y_part, 2 * g + 2) if g < NF // 2 - 1 else (y_mm, KT),
                                   (NF // 2 + g + 2) % STAGE) for g in range(NF // 2)]
        assert len(fills) == MOE0
        assert [expert_slot(k) for k in range(SLOTS)] == slot_of[-SLOTS:]
        level = [0] * SLOTS
        landed = []
        freed = []
        last = {}
        for n, (parts, free) in enumerate(fills):
            sl = slot_of[n]
            level[sl] += 16 * len(parts)
            landed.append(level[sl])
            if sl == STAGE and sl in last and last[sl] < F[0]["w2"][0] < n:
                freed.append((y_mm, KT))
            else:
                freed.append(fills[last[sl]][1] if sl in last else None)
            last[sl] = n

        def arrived(eng, n):
            eng.wait_ge(filled[slot_of[n]], landed[n])

        stage = slot_r[STAGE]
        h_hi = [stage[:, k * TT:(k + 1) * TT] for k in range(KT)]
        h_lo = [hT_r[:, k * TT:(k + 1) * TT] for k in range(KT)]
        piece_hi = [stage[:, 4096 + i * D:4096 + (i + 1) * D].rearrange("p (k n) -> p k n", k=KT) for i in range(2)]
        f2_hi = [slot_r[0][:, 4096 + i * D:4096 + (i + 1) * D] for i in range(2)]
        a_hi = [slot_r[1][:, 4096 + i * TT:4096 + (i + 1) * TT] for i in range(2)]
        a_lo = [scr_r[:, i * TT:(i + 1) * TT] for i in range(16)] + \
               [tail_r[:, i * TT:(i + 1) * TT] for i in range(6)]

        def piece(h, halves=False):
            n, half = divmod(h, 2)
            return slot(F[0]["w13"][n // 2], KT, 256, half * KT * 256, halves)[:, :, (n % 2) * P:(n % 2 + 1) * P]

        def f2_row(n, halves=False):
            return slot(F[0]["w2"][n // 2], 2, D, 0, halves)[:, n % 2, :]

        def piece_count(h):
            return h + 1 if h < 2 else KT + h + 1

        def h_count(k):
            return 3 + k

        def second_count(n, a):
            return KT + 2 * NF + 2 * n + 1 + a

        def units(l):
            u = [(c, hh, qt, 0, 0) for c in range(NC) for hh in range(2) for qt in range(2)]
            if l == 0:
                u += [(c, hh, qt, 2, 1) for c in range(NC) for hh in range(2) for qt in range(2)]
            return u

        segs = [[0, 1], [0]]

        def rounds(eng, body):
            body(0)
            eng.wait_ge(most_ready, 1)
            n = eng.value_load(most[0:1, 0:1], min_val=0, max_val=S)
            for r in range(1, ROUNDS):
                with eng.If(n > r * C):
                    body(r)

        block = ctx.enter_context(nc.Block())

        @block.sync
        def _(sp):
            sp.dma_start(rows[0:48, 0:P], t["b_ada"][0].rearrange("(a p) -> a p", p=P)).then_inc(rows_in, 16)
            sp.dma_start(rows[48:96, 0:P], t["b_ada"][1].rearrange("(a p) -> a p", p=P)).then_inc(rows_in, 16)
            sp.dma_start(rows[96:104, 0:P], t["c"].rearrange("b (a p) -> (b a) p", p=P)).then_inc(rows_in, 16)
            sp.dma_start(rows[104:112, 0:P], t["c_ctx"].rearrange("(a p) -> a p", p=P)).then_inc(rows_in, 16)
            sp.dma_start(rows[112:120, 0:P], t["final_g"].rearrange("(a p) -> a p", p=P)).then_inc(rows_in, 16)
            at = 0
            for name, n in [("norm1_g", 16), ("norm2_g", 16), ("dw_b", 8), ("conv_ln_g", 8), ("conv_ln_b", 8)]:
                sp.dma_start(rows[at:at + n, P:2 * P],
                             t[name].rearrange("l (a p) -> (l a) p", p=P)).then_inc(rows_in, 16)
                at += n
            for l in range(2):
                sp.dma_start(rows[0:TAPS * NC, (2 + l) * P:(3 + l) * P],
                             t["dw_w"][l].rearrange("k (a p) -> (k a) p", p=P)).then_inc(rows_in, 16)
            for n, (parts, free) in enumerate(fills):
                if n >= SLOTS:
                    sp.wait_ge(*freed[n])
                for dst, src in parts:
                    sp.dma_start(dst, src).then_inc(filled[slot_of[n]], 16)

            def expert_fill(k, e):
                s = expert_slot(k)
                w = tiles_in(k) * P
                a, f = OFF[s], FIRST[k] * P
                for i, name in enumerate(["exp_w1", "exp_w3"]):
                    src = t[name][0, e].rearrange("(k p) n -> p k n", p=P)[:, :, f:f + w]
                    dst = ring[:, a + i * KT * w:a + (i + 1) * KT * w].rearrange("p (k n) -> p k n", k=KT)
                    sp.dma_start(dst, src).then_inc(filled[s], 16)
                src = t["exp_w2"][0, e][f:f + w, :].rearrange("(k p) n -> p k n", p=P)
                dst = ring[:, a + 2 * KT * w:a + 3 * KT * w].rearrange("p (k n) -> p k n", n=D)
                sp.dma_start(dst, src).then_inc(filled[s], 16)

            def expert_weights(r):
                base = NE * r
                for k in range(SLOTS):
                    if r == 0:
                        n = MOE0 + k - SLOTS
                        sp.wait_ge(*fills[n][1])
                        if expert_slot(k) == SLOTS - 1:
                            sp.wait_ge(L[1]["mix_ready"], NC)
                    else:
                        sp.wait_ge(w2_mm, NF * (base - 1) + FIRST[k + SLOTS + 1])
                    expert_fill(k, 0)
                with sp.Fori(0, NE - 1) as e:
                    for k in range(SLOTS, 2 * SLOTS):
                        sp.wait_ge(w2_mm, NF * e + (NF * base + FIRST[k - SLOTS + 1]))
                        expert_fill(k, e)
                    for k in range(SLOTS):
                        sp.wait_ge(w2_mm, NF * e + (NF * base + FIRST[k + SLOTS + 1]))
                        expert_fill(k, e + 1)
                for k in range(SLOTS, 2 * SLOTS):
                    sp.wait_ge(w2_mm, NF * (base + NE - 1) + FIRST[k - SLOTS + 1])
                    expert_fill(k, NE - 1)

            rounds(sp, expert_weights)
            for n in range(2):
                sp.wait_ge(ot_ready, 2 * n + 2)
                sp.dma_start(out[0, n * P:(n + 1) * P, :], otok[:, 2 + n, :]).then_inc(stored, 16)
            sp.wait_ge(stored, 32)

        @block.tensor
        def _(pe):
            mm = pe.matmul
            pe.wait_ge(const_in, 16)
            pe.wait_ge(rows_in, 16 * 12)
            pe.transpose(bank[7][:, 0:120], rows[0:120, 0:P], ident[0:120, 0:120])
            pe.transpose(bank[7][:, 120:176], rows[0:56, P:2 * P], ident[0:56, 0:56])
            pe.transpose(bank[7][:, 176:300], rows[0:124, 2 * P:3 * P], ident[0:124, 0:124])
            pe.transpose(bank[7][:, 300:424], rows[0:124, 3 * P:4 * P], ident[0:124, 0:124]).then_inc(vec_mm, 1)
            pe.wait_ge(x_in, 32)
            for c in range(KT):
                if c >= 2:
                    pe.wait_ge(xt_ready, c - 1)
                for n in range(4):
                    i = pe.transpose(bank[c % 2][:, n * P:(n + 1) * P], xtok[:, n, c * P:(c + 1) * P], ident)
                i.then_inc(xt_mm, 1)

            def modulate(l, b):
                m = L[l]
                if b:
                    pe.wait_ge(m["mod_row"], b)
                for n in range(4):
                    arrived(pe, F[l]["ada"][4 * b + n])
                    w = slot(F[l]["ada"][4 * b + n], KT, 512)
                    for k in range(KT):
                        for j in range(4):
                            i = mm(bank[6][32 * j:32 * j + 32, n * P:(n + 1) * P], silu_c[:, 2 * k:2 * k + 32],
                                   w[:, k, j * P:(j + 1) * P], start=(k == 0), stop=(k == KT - 1))
                    i.then_inc(m["mod_mm"], 1)

            def turn_modulation(l, b):
                m = L[l]
                pe.wait_ge(m["mod_row"], b + 1)
                if b:
                    pe.wait_ge(m["mod_done"], b)
                for n in range(4):
                    i = pe.transpose(bank[7][:, n * P:(n + 1) * P], mrow[b % 2][:, n * P:(n + 1) * P], ident)
                i.then_inc(m["mod_t"], 1)

            def norm_stats(sq, st, T):
                for k in range(KT):
                    pe.wait_ge(sq, k + 1)
                    i = mm(bank[4][:, 0:T], const("mean_d"), hv[:, k, 0:T], start=(k == 0), stop=(k == KT - 1))
                i.then_inc(st, 1)

            for l in range(2):
                m = L[l]
                ns = len(segs[l])
                TQ = ns * S
                if l == 0:
                    norm_stats(m["sq1"], m["st1"], TT)
                    pe.wait_ge(silu_ready, 2)
                    modulate(l, 0)
                else:
                    pe.wait_ge(x2, 2 * 4)
                    modulate(l, 0)
                    pe.wait_ge(x2, 2 * KT)
                    norm_stats(m["sq1"], m["st1"], TT)
                turn_modulation(l, 0)
                pe.wait_ge(m["h1_ready"], 2 * KT)
                arrived(pe, F[l]["qkv"])
                w = slot(F[l]["qkv"], KT, 768)
                for i_ in range(7):
                    if i_ < 5:
                        j = i_
                        T = TQ if j < 4 else TT
                        if j >= 2:
                            pe.wait_ge(m["qk_sq"], j - 1)
                            pe.wait_ge(m["qk_raw"], j - 1)
                        for k in range(KT):
                            i = mm(bank[j % 2][:, 0:T], w[:, k, j * P:(j + 1) * P], hv[:, k, 0:T],
                                   start=(k == 0), stop=(k == KT - 1))
                        i.then_inc(m["qk_mm"], 1)
                    j = i_ - 1
                    if 0 <= j < 5:
                        T = TQ if j < 4 else TT
                        pe.wait_ge(m["qk_sq"], j + 1)
                        if j >= 2:
                            pe.wait_ge(m["qk_rstd"], j - 1)
                        mm(bank[2 + j % 2][:, 0:T], const("mean_head"), tmpA[j % 2][:, 0:T],
                           start=True, stop=True).then_inc(m["qk_stat"], 1)
                    j = i_ - 2
                    if 0 <= j < 5:
                        pe.wait_ge(m["qk_norm"], j + 1)
                        if j >= 2:
                            pe.wait_ge(m["roped"], j - 1)
                        mm(bank[4 + j % 2][:, 0:S], const("rot"), qn[j][:, 0:S],
                           start=True, stop=True).then_inc(m["qk_rot"], 1)
                for n in range(4):
                    for k in range(KT):
                        i = mm(bank[7][:, n * P:(n + 1) * P], hv[:, k, n * P:(n + 1) * P], w[:, k, 640:768],
                               start=(k == 0), stop=(k == KT - 1))
                i.then_inc(m["v_mm"], 1)
                for c in range(NC):
                    arrived(pe, F[l]["u"][c // 2])
                    w = slot(F[l]["u"][c // 2], 2 * KT, 256)
                    if c == 0:
                        pe.wait_ge(m["qk_raw"], 5)
                        pe.wait_ge(m["qk_sq"], 5)
                        pe.wait_ge(m["qk_rstd"], 5)
                    if c >= 2:
                        pe.wait_ge(m["glu"], c - 1)
                    for half in range(2):
                        for k in range(KT):
                            i = mm(bank[2 * half + c % 2][:, 0:TQ],
                                   w[:, half * KT + k, (c % 2) * P:(c % 2 + 1) * P], hv[:, k, 0:TQ],
                                   start=(k == 0), stop=(k == KT - 1))
                    i.then_inc(m["u_mm"], 1)
                pe.wait_ge(m["roped"], 5)
                mm(bank[5][:, :], const("halves"), qn[4], start=True, stop=True).then_inc(m["ks_mm"], 1)
                pe.wait_ge(m["v_ready"], 1)
                modulate(l, 1)
                turn_modulation(l, 1)
                modulate(l, 2)
                turn_modulation(l, 2)
                U = units(l)
                pe.wait_ge(m["glu"], NC)
                pe.wait_ge(m["ks_ready"], 1)
                pe.wait_ge(m["mod_done"], 3)
                per = -(-TAPS // len(U))
                k = 0
                def score(u):
                    c, hh, qt, k0, sg = U[u]
                    if u >= 2:
                        pe.wait_ge(m["exp_done"], u - 1)
                    key = qn[4] if c // 2 == hh else kswap
                    p0 = HD * hh
                    q0 = sg * S + qt * P
                    mm(bank[u % 2][:, 0:TT - k0 * P], qn[c][p0:p0 + HD, q0:q0 + P], key[p0:p0 + HD, k0 * P:TT],
                       start=True, stop=True).then_inc(m["sc_mm"], 1)

                score(0)
                for st in range(len(U) + 2):
                    u = st - 1
                    if 0 <= u < len(U):
                        nk = 4 - U[u][3]
                        pe.wait_ge(m["diag_ready"], u + 1)
                        if u >= 2:
                            pe.wait_ge(m["pt_ready"], u - 1)
                        for kt in range(nk):
                            i = mm(bank[2 + u % 2][:, kt * P:(kt + 1) * P], tmpA[u % 2][:, kt * P:(kt + 1) * P],
                                   diag[u % 2], start=True, stop=True)
                        i.then_inc(m["pt_mm"], 1)
                    if st + 1 < len(U):
                        score(st + 1)
                    for _ in range(per):
                        if k < TAPS:
                            pe.wait_ge(m["cd_ready"], k + 1)
                            mm(bank[7][:, 0:TQ].rearrange("p (s t) -> p s t", s=ns), cdiag[k % 4],
                               ypad[:, 3, 0:ns, k:k + S], start=(k == 0), stop=(k == TAPS - 1)
                               ).then_inc(m["cd_mm"], 1)
                        k += 1
                    u = st - 2
                    if 0 <= u < len(U):
                        c, hh, qt, k0, sg = U[u]
                        kv = c // 2
                        nk = 4 - k0
                        pe.wait_ge(m["pt_ready"], u + 1)
                        ci = u // 4
                        if u % 4 == 0 and ci >= 2:
                            pe.wait_ge(m["o_ready"], ci - 1)
                        for kt in range(nk):
                            i = mm(bank[4 + ci % 2][HD * hh:HD * hh + HD, qt * P:(qt + 1) * P],
                                   vtok[:, k0 + kt, kv * HD:(kv + 1) * HD], tmpB[u % 2][:, kt * P:(kt + 1) * P],
                                   start=(kt == 0), stop=(kt == nk - 1))
                        i.then_inc(m["pv_mm"], 1)
                pe.wait_ge(m["conv_step"], 3 * TAPS)
                pe.wait_ge(m["conv3"], 1)
                for c in range(NC):
                    i = mm(bank[7][:, 0:TQ], const("mean_conv"), acc[c][:, 0:TQ], start=(c == 0), stop=(c == 3))
                i.then_inc(m["mean_mm"], 1)
                for c in range(NC):
                    pe.wait_ge(m["ln_sq"], c + 1)
                    i = mm(bank[6][:, 0:TQ], const("mean_conv"), (tmpA + tmpB)[c][:, 0:TQ],
                           start=(c == 0), stop=(c == 3))
                i.then_inc(m["var_mm"], 1)
                pe.wait_ge(m["exp_done"], len(U))
                pe.wait_ge(m["pt_ready"], len(U))
                pe.wait_ge(m["o_ready"], len(U) // 4)
                pe.wait_ge(m["mix_ready"], NC)
                for j in range(KT):
                    arrived(pe, F[l]["wo"][j // 4])
                    w = slot(F[l]["wo"][j // 4], KT, 512)
                    if j >= 4:
                        pe.wait_ge(m["x1"], ns * (j - 3))
                    for k in range(KT):
                        i = mm(bank[j % 4][:, 0:TQ], w[:, k, (j % 4) * P:(j % 4 + 1) * P], hv[:, k, 0:TQ],
                               start=(k == 0), stop=(k == KT - 1))
                    i.then_inc(m["wo_mm"], 1)
                norm_stats(m["sq2"], m["st2"], TQ)
                pe.wait_ge(m["x1"], ns * KT)
                pe.wait_ge(m["h2_ready"], ns * KT)
                if l == 0:
                    for n in range(NF):
                        if n >= 2:
                            pe.wait_ge(a_ready, n - 1)
                        for half in range(2):
                            h = 2 * n + half
                            b = bank[2 * half + n % 2][:, :]
                            pe.wait_ge(lo_ready, piece_count(h))
                            for k in range(KT):
                                if h == 0:
                                    pe.wait_ge(lo_ready, h_count(k))
                                hi, lo = piece_hi[h % 2][:, k, :], piece(h, True)[:, k, :]
                                mm(b, hi, h_hi[k], start=(k == 0), stop=False)
                                mm(b, hi, h_lo[k], start=False, stop=False)
                                i = mm(b, lo, h_hi[k], start=False, stop=(k == KT - 1))
                            i.then_inc(f_mm, 1)
                    for n in range(NF):
                        pe.wait_ge(lo_ready, second_count(n, 1))
                        for d in range(KT):
                            if n == 0 and d == 4:
                                pe.wait_ge(a_ready, NF)
                            b = bank[(d + 4) % 8][:, :]
                            hi = f2_hi[n % 2][:, d * P:(d + 1) * P]
                            lo = f2_row(n, True)[:, d * P:(d + 1) * P]
                            mm(b, hi, a_hi[n % 2], start=(n == 0), stop=False)
                            mm(b, hi, a_lo[n], start=False, stop=False)
                            i = mm(b, lo, a_hi[n % 2], start=False, stop=(n == NF - 1))
                            if n == NF - 1:
                                i.then_inc(y_mm, 1)
                        if n < NF - 1:
                            i.then_inc(y_part, 1)

            for b in range(4):
                for c in range(4):
                    k = (b % 2) * 4 + c
                    i = pe.transpose(bank[b][:, c * P:(c + 1) * P],
                                     hv[:, k, (b // 2) * P:(b // 2 + 1) * P], ident)
                i.then_inc(tok_mm, 1)
            pe.wait_ge(rows_in, 16 * 12)
            pe.wait_ge(vec_in, 16 * 10)
            for n in range(2):
                for k in range(KT):
                    i = mm(bank[4][:, n * NE:(n + 1) * NE], hv[:, k, n * P:(n + 1) * P],
                           rw[:, k * NE:(k + 1) * NE], start=(k == 0), stop=(k == KT - 1))
            i.then_inc(lg_mm, 1)
            pe.wait_ge(mask_ready, 1)
            mask = [small[:, 0:NE], small[:, NE:2 * NE]]
            mm(bank[5][:, 0:NE], const("before"), mask[0], start=True, stop=True)
            mm(bank[5][:, NE:2 * NE], const("before"), mask[1], start=True, stop=False)
            mm(bank[5][:, NE:2 * NE], const("ones"), mask[0], start=False, stop=True)
            mm(bank[5][:, 2 * NE:3 * NE], const("ones"), mask[0], start=True, stop=False)
            mm(bank[5][:, 2 * NE:3 * NE], const("ones"), mask[1], start=False, stop=True).then_inc(pos_mm, 1)
            pe.wait_ge(tok_ready, 4)
            pe.wait_ge(pos_ready, 1)

            def gather(at):
                pe.wait_ge(sel_ready, at(1))
                for half in range(2):
                    for c in range(4):
                        for n in range(2):
                            k = half * 4 + c
                            i = mm(bank[4 + half][:, c * C:(c + 1) * C], h2tok[:, n, k * P:(k + 1) * P],
                                   sel[:, n, :], start=(n == 0), stop=(n == 1))
                    i.then_inc(g_mm, 1)

            def scatter(at):
                for pr in range(4):
                    if pr >= 2:
                        pe.wait_ge(acc_done, at(pr))
                    for c in range(2):
                        k = 2 * pr + c
                        i = mm(bank[6 + pr % 2][:, c * S:(c + 1) * S], ytok[:, k * P:(k + 1) * P], sgT,
                               start=True, stop=True)
                    i.then_inc(sc_e, 1)

            def expert(e, r):
                def at(v, per=NF, steps=NE):
                    return per * e + (per * steps * r + v)

                def second(n):
                    b = n % 2
                    pe.wait_ge(ea_ready, at(n + 3))
                    if n == 0:
                        pe.wait_ge(ytok_ready, at(1, 2))
                    for d in range(2):
                        cols = slice(d * 512, (d + 1) * 512)
                        for part, (x, w2) in enumerate([(ae_hi, w2_hi), (ae_hi, w2_lo), (ae_lo, w2_hi)]):
                            i = mm(bank[2 + d][0:C, :], x[b], w2[b][:, cols],
                                   start=(n == 0 and part == 0), stop=(n == NF - 1 and part == 2))
                    i.then_inc(w2_mm, 1)

                pe.wait_ge(xg_ready, at(2, 2, NE + 1))
                prev = None
                for k in range(2 * SLOTS):
                    s = expert_slot(k)
                    w = tiles_in(k) * P
                    a = OFF[s]
                    pe.wait_ge(filled[s], at(level[s] + 48 * (k // SLOTS + 1), 96))
                    for j in range(tiles_in(k)):
                        n = FIRST[k] + j
                        pe.wait_ge(ea_ready, at(n + 1))
                        for half in range(2):
                            for q in range(KT):
                                col = a + (half * KT + q) * w + j * P
                                i = mm(bank[n % 2][:, half * C:(half + 1) * C], ring[:, col:col + P], xg[:, q, :],
                                       start=(q == 0), stop=(q == KT - 1))
                        i.then_inc(eh_mm, 1)
                        if n == NF - 1:
                            gather(lambda v: at(v + 1, 1, NE + 1))
                        if prev is not None:
                            second(prev)
                        prev = n
                        if n == 3:
                            pe.wait_ge(acc_done, at(1, 4, NE + 1))
                            scatter(lambda v: at(v, 4, NE + 1))
                        if n == 8:
                            pe.wait_ge(acc_done, at(5, 4, NE + 1))
                            for q in range(2):
                                i = pe.transpose(bank[6][0:C, q * P:(q + 1) * P], selg[:, q, :], ident)
                            i.then_inc(st_mm, 1)
                second(prev)

            def experts(r):
                gather(lambda v: (NE + 1) * r + v)
                pe.wait_ge(sgt_zero, r + 1)
                with pe.Fori(0, NE) as e:
                    expert(e, r)
                pe.wait_ge(ytok_ready, 2 * NE * (r + 1) + 1)
                pe.wait_ge(acc_done, 4 * (NE + 1) * r + 4 * NE + 1)
                scatter(lambda v: 4 * (NE + 1) * r + 4 * NE + v)

            rounds(pe, experts)

            for k in range(KT):
                pe.wait_ge(sqf, k + 1)
                i = mm(bank[4][:, 0:S], const("mean_d"), hv[:, k, 0:S], start=(k == 0), stop=(k == KT - 1))
            i.then_inc(stf, 1)
            pe.wait_ge(outn, KT)
            for b in range(4):
                for c in range(4):
                    k = (b % 2) * 4 + c
                    i = pe.transpose(bank[b][:, c * P:(c + 1) * P], hv[:, k, (b // 2) * P:(b // 2 + 1) * P], ident)
                i.then_inc(ot_mm, 1)

        @block.scalar
        def _(act):
            act.dma_start(con[:, :], t["constants"]).then_inc(const_in, 16)
            act.dma_start(xtok[:, 0:2, :], t["x"][0].rearrange("(n p) d -> p n d", p=P)).then_inc(x_in, 16)
            act.dma_start(xtok[:, 2:4, :], t["ctx"][0].rearrange("(n p) d -> p n d", p=P)).then_inc(x_in, 16)
            for l in range(2):
                for i, name in enumerate(["q_norm_g", "k_norm_g"]):
                    for h in range(2):
                        act.dma_start(qk_g[h * HD:(h + 1) * HD, 2 * l + i:2 * l + i + 1],
                                      t[name][l].rearrange("(p a) -> p a", a=1)).then_inc(vec_in, 16)
            act.dma_start(rw[:, :].rearrange("p (k e) -> p k e", k=KT),
                          t["router_w"][0].rearrange("(k p) e -> p k e", p=P)).then_inc(vec_in, 16)
            act.dma_start(rb[:, :], t["router_b"][0:1, :].to_broadcast([P, NE])).then_inc(vec_in, 16)
            f = act.activation

            def root(dst, bank_, T, stat, n, done):
                act.wait_ge(stat, n)
                f(dst[:, 0:T], bank_[:, 0:T], ACT.Sqrt, bias=eps[:, 0:1]).then_inc(done, 1)

            act.wait_ge(eps_ready, 1)
            act.wait_ge(vec_ready, 1)
            for v in range(2):
                f(silu_cv[:, :, v], vec1[:, 96 + 8 * v:104 + 8 * v], ACT.Silu).then_inc(silu_ready, 1)

            def modulation_rows(m, b):
                act.wait_ge(m["mod_mm"], 4 * b + 4)
                if b == 2:
                    act.wait_ge(m["mod_t"], 1)
                f(mrow[b % 2], bank[6][:, :], ACT.Copy).then_inc(m["mod_row"], 1)

            for c in range(KT):
                act.wait_ge(xt_mm, c + 1)
                f(xv[:, c, :], bank[c % 2][:, :], ACT.Copy).then_inc(xt_ready, 1)

            def shift(m, l, which, done, ready):
                n = 0
                for c in range(KT):
                    for sg in ([0, 1] if which == 0 else segs[l]):
                        act.wait_ge(m[done], n + 1)
                        h = hv[:, c, sg * S:(sg + 1) * S]
                        f(h, h, ACT.Identity, bias=mods[l][:, 24 * which + c, sg:sg + 1]).then_inc(m[ready], 1)
                        n += 1
                    if which == 1 and l == 0:
                        act.wait_ge(m[ready], n)
                        f(h_hi[c], hv[:, c, :], ACT.Copy).then_inc(hi_ready, 1)

            def piece_halves(h):
                if h >= 2:
                    act.wait_ge(f_mm, h - 1)
                if h % 4 == 0:
                    arrived(act, F[0]["w13"][h // 4])
                f(piece_hi[h % 2], piece(h), ACT.Copy).then_inc(hi_ready, 1)

            def second_halves(n):
                if n >= 2:
                    act.wait_ge(y_part, n - 1)
                if n % 2 == 0:
                    arrived(act, F[0]["w2"][n // 2])
                f(f2_hi[n % 2], f2_row(n), ACT.Copy).then_inc(hi_ready, 1)
                act.wait_ge(a_ready, n + 1)
                f(a_hi[n % 2], aT[n], ACT.Copy).then_inc(hi_ready, 1)

            for l in range(2):
                m = L[l]
                ns = len(segs[l])
                TQ = ns * S
                if l == 0:
                    act.wait_ge(xt_mm, KT)
                    act.wait_ge(xt_ready, KT)
                for c in range(KT):
                    if l == 1:
                        act.wait_ge(x2, 2 * c + 2)
                    f(hv[:, c, :], xv[:, c, :], ACT.Square).then_inc(m["sq1"], 1)
                if l == 0:
                    root(rstd, bank[4], TT, m["st1"], 1, m["root"])
                    modulation_rows(m, 0)
                else:
                    modulation_rows(m, 0)
                    root(rstd, bank[4], TT, m["st1"], 1, m["root"])
                act.wait_ge(m["mod_done"], 1)
                shift(m, l, 0, "scaled1", "h1_ready")
                for st in range(6):
                    j = st
                    if j < 5:
                        T = TQ if j < 4 else TT
                        act.wait_ge(m["qk_mm"], j + 1)
                        if j >= 2:
                            act.wait_ge(m["qk_stat"], j - 1)
                        f(tmpA[j % 2][:, 0:T], bank[j % 2][:, 0:T], ACT.Square).then_inc(m["qk_sq"], 1)
                    j = st - 1
                    if j >= 0:
                        if j == 0:
                            act.wait_ge(m["scaled1"], 2 * KT)
                        else:
                            act.wait_ge(m["qk_norm"], j)
                        root(rstd, bank[2 + j % 2], TQ if j < 4 else TT, m["qk_stat"], j + 1, m["root"])
                act.wait_ge(m["v_mm"], 1)
                f(scr[:, 3072:3584], bank[7][:, :], ACT.Copy).then_inc(m["v_ready"], 1)
                act.wait_ge(m["qk_stat"], 5)
                for c in range(NC):
                    act.wait_ge(m["u_mm"], c + 1)
                    if c >= 2:
                        act.wait_ge(m["glu"], c - 1)
                    f(tmpA[c % 2][:, 0:TQ], bank[2 + c % 2][:, 0:TQ], ACT.Sigmoid).then_inc(m["u_sig"], 1)
                act.wait_ge(m["ks_mm"], 1)
                f(kswap, bank[5][:, :], ACT.Copy).then_inc(m["ks_ready"], 1)
                modulation_rows(m, 1)
                modulation_rows(m, 2)
                U = units(l)
                act.wait_ge(m["glu"], NC)
                act.wait_ge(m["roped"], 5)
                per = -(-TAPS // len(U))
                k = 0
                for st in range(len(U) + 2):
                    for _ in range(per):
                        if k < TAPS:
                            if k >= 4:
                                act.wait_ge(m["cd_mm"], k - 3)
                            f(cdiag[k % 4], ident, ACT.Copy, scale=dwt[:, 124 * l + 4 * k + 3:124 * l + 4 * k + 4]
                              ).then_inc(m["cd_ready"], 1)
                        k += 1
                    if st < len(U):
                        act.wait_ge(m["nb_ready"], st + 1)
                        if st >= 2:
                            act.wait_ge(m["pt_mm"], st - 1)
                        n = TT - U[st][3] * P
                        f(tmpA[st % 2][:, 0:n], bank[st % 2][:, 0:n], ACT.Exp, bias=att[:, 32 + st:33 + st],
                          scale=HD ** -0.5, accum_out=att[:, 64 + st:65 + st]).then_inc(m["exp_done"], 1)
                    u = st - 1
                    if 0 <= u < len(U):
                        n = TT - U[u][3] * P
                        act.wait_ge(m["pt_mm"], u + 1)
                        if u >= 2:
                            act.wait_ge(m["pv_mm"], u - 1)
                        f(tmpB[u % 2][:, 0:n], bank[2 + u % 2][:, 0:n], ACT.Copy).then_inc(m["pt_ready"], 1)
                    u = st - 2
                    if 0 <= u < len(U) and u % 4 == 3:
                        c, _, _, _, sg = U[u]
                        act.wait_ge(m["pv_mm"], u + 1)
                        f(hv[:, c, sg * S:(sg + 1) * S], bank[4 + (u // 4) % 2][:, 0:S],
                          ACT.Copy).then_inc(m["o_ready"], 1)
                act.wait_ge(m["pt_mm"], len(U))
                act.wait_ge(m["pv_mm"], len(U))
                for c in range(NC):
                    act.wait_ge(m["centred"], c + 1)
                    f((tmpA + tmpB)[c][:, 0:TQ], acc[c][:, 0:TQ], ACT.Square).then_inc(m["ln_sq"], 1)
                root(rstd, bank[6], TQ, m["var_mm"], 1, m["root"])
                for c in range(NC):
                    act.wait_ge(m["ln_scaled"], c + 1)
                    f(hv[:, NC + c, 0:TQ], acc[c][:, 0:TQ], ACT.Silu, bias=vec2[:, 48 + 4 * l + c:49 + 4 * l + c],
                      scale=vec2[:, 40 + 4 * l + c:41 + 4 * l + c]).then_inc(m["mix_ready"], 1)
                if l == 0:
                    piece_halves(0)
                    piece_halves(1)
                act.wait_ge(m["wo_mm"], KT)
                for c in range(KT):
                    act.wait_ge(m["x1"], ns * (c + 1))
                    f(hv[:, c, 0:TQ], xv[:, c, 0:TQ], ACT.Square).then_inc(m["sq2"], 1)
                act.wait_ge(m["ln_scaled"], NC)
                root(rstd, bank[4], TQ, m["st2"], 1, m["root"])
                shift(m, l, 1, "scaled2", "h2_ready")
                if l == 0:
                    for n in range(NF):
                        if n == NF - 1:
                            second_halves(0)
                            second_halves(1)
                        act.wait_ge(f_mm, 2 * n + 1)
                        f(aT[n], bank[n % 2][:, :], ACT.Silu).then_inc(f_silu, 1)
                        if n < NF - 1:
                            piece_halves(2 * n + 2)
                            piece_halves(2 * n + 3)
                    for n in range(2, NF):
                        second_halves(n)

            for b in range(4):
                act.wait_ge(tok_mm, b + 1)
                f(scr[:, b * 512:(b + 1) * 512], bank[b][:, :], ACT.Copy).then_inc(tok_ready, 1)
            for n in range(2):
                act.wait_ge(dm_ready, n + 1)
                f(rt[:, 80 * n + 74:80 * n + 75], rt[:, 80 * n + 73:80 * n + 74], ACT.Exp).then_inc(ed_ready, 1)

            def gathered(at):
                for half in range(2):
                    act.wait_ge(g_mm, at(half + 1))
                    f(scr[:, 4096 + half * 4 * C:4096 + (half + 1) * 4 * C], bank[4 + half][:, 0:4 * C],
                      ACT.Copy).then_inc(xg_ready, 1)

            def expert(e, r):
                def at(v, per=NF, steps=NE):
                    return per * e + (per * steps * r + v)

                for n in range(NF):
                    if n in FIRST:
                        k = FIRST.index(n)
                        sl = expert_slot(k)
                        act.wait_ge(filled[sl], at(level[sl] + 48 * (k // SLOTS + 1), 96))
                    if n >= 2:
                        act.wait_ge(w2_mm, at(n - 1))
                    f(w2_hi[n % 2], w2_row(n), ACT.Copy).then_inc(w2hi_ready, 1)
                    act.wait_ge(eh_mm, at(n + 1))
                    act.wait_ge(ea_ready, at(n + 1))
                    f(ae[n % 2], bank[n % 2][:, 0:C], ACT.Silu).then_inc(e_silu, 1)
                    act.wait_ge(prod, at(n + 1))
                    f(ae_hi[n % 2], ae[n % 2], ACT.Copy).then_inc(ahi_ready, 1)
                    if n == 10:
                        act.wait_ge(st_mm, at(2, 1))
                        f(sgT, bank[6][0:C, 0:S], ACT.Copy).then_inc(sgt_ready, 1)
                gathered(lambda v: at(v + 2, 2, NE + 1))
                act.wait_ge(w2_mm, at(NF))
                for half in range(2):
                    f(ytok[:, half * 512:(half + 1) * 512], bank[2 + half][0:C, :],
                      ACT.Copy).then_inc(ytok_ready, 1)

            def experts(r):
                gathered(lambda v: 2 * (NE + 1) * r + v)
                with act.Fori(0, NE) as e:
                    expert(e, r)

            rounds(act, experts)
            for c in range(KT):
                act.wait_ge(xf, c + 1)
                f(hv[:, c, 0:S], xv[:, c, 0:S], ACT.Square).then_inc(sqf, 1)
            root(frstd, bank[4], S, stf, 1, rootf)
            for b in range(4):
                act.wait_ge(ot_mm, b + 1)
                f(otok[:, 2 + b // 2, (b % 2) * 512:(b % 2 + 1) * 512], bank[b][:, :],
                  ACT.Copy).then_inc(ot_ready, 1)

        @block.vector
        def _(dve):
            chain = [0]

            def link(ins):
                chain[0] += 1
                ins.then_inc(dve_chain, 1)
                dve.wait_ge(dve_chain, chain[0])

            ts, tt, stt = dve.tensor_scalar, dve.tensor_tensor, dve.scalar_tensor_tensor
            link(dve.memset(silu_c[:, :], 0.0))
            dve.memset(eps[:, :], EPS).then_inc(eps_ready, 1)
            dve.wait_ge(vec_mm, 1)
            dve.tensor_copy(vec1[:, :], bank[7][:, 0:120])
            dve.tensor_copy(vec2[:, :], bank[7][:, 120:176])
            dve.tensor_copy(dwt[:, :], bank[7][:, 176:424]).then_inc(vec_ready, 1)
            dve.wait_ge(vec_ready, 1)

            def scale(m, l, which, src, done, T):
                for c in range(KT):
                    for sg in range(T // S):
                        x = xv[:, c, sg * S:(sg + 1) * S]
                        stt(out=hv[:, c, sg * S:(sg + 1) * S], in0=x, scalar=gains[l][which][:, c, sg:sg + 1],
                            in1=rstd[:, sg * S:(sg + 1) * S], op0=ALU.mult, op1=ALU.mult).then_inc(m[done], 1)

            def residual(ps, l, c, gate, sg, done):
                x = xv[:, c, sg * S:(sg + 1) * S]
                stt(out=x, in0=ps[:, sg * S:(sg + 1) * S], scalar=mods[l][:, gate + c, sg:sg + 1],
                    in1=x, op0=ALU.mult, op1=ALU.add).then_inc(done, 1)

            def piece_rest(h):
                dve.wait_ge(hi_ready, piece_count(h))
                tt(piece(h, True), piece(h), piece_hi[h % 2].bitcast(F32), ALU.subtract).then_inc(lo_ready, 1)

            def second_rest(n):
                dve.wait_ge(hi_ready, second_count(n, 0))
                tt(f2_row(n, True), f2_row(n), f2_hi[n % 2].bitcast(F32), ALU.subtract).then_inc(lo_ready, 1)
                dve.wait_ge(hi_ready, second_count(n, 1))
                tt(a_lo[n], aT[n], a_hi[n % 2].bitcast(F32), ALU.subtract).then_inc(lo_ready, 1)

            def modulation(l, b):
                m = L[l]
                dve.wait_ge(m["mod_t"], b + 1)
                lo = 16 * b
                bias = vec1[:, l * 48 + lo:l * 48 + lo + 16].rearrange("p (m v) -> p m v", v=1).to_broadcast([P, 16, 2])
                ps = bank[7][:, :].rearrange("p (m q) -> p m q", q=32)[:, :, 0:2]
                link(tt(mods[l][:, lo:lo + 16, :], ps, bias, ALU.add))
                which, s0 = {0: (0, 8), 1: (0, 8), 2: (1, 32)}[b]
                g = vec2[:, 16 * which + 8 * l:16 * which + 8 * l + 8]
                g = g.rearrange("p (m v) -> p m v", v=1).to_broadcast([P, KT, 2])
                stt(out=gains[l][which], in0=mods[l][:, s0:s0 + 8, :], scalar=1.0, in1=g,
                    op0=ALU.add, op1=ALU.mult).then_inc(m["mod_done"], 1)
                dve.wait_ge(m["mod_done"], b + 1)

            for l in range(2):
                m = L[l]
                ns = len(segs[l])
                TQ = ns * S
                dve.wait_ge(m["root"], 1)
                link(dve.reciprocal(rstd[:, 0:TT], rstd[:, 0:TT]))
                modulation(l, 0)
                if l == 0:
                    dve.wait_ge(xt_ready, KT)
                scale(m, l, 0, "x", "scaled1", TT)
                dve.memset(ypad[:, :, :, 0:PAD], 0.0)
                link(dve.memset(ypad[:, :, :, PAD + S:], 0.0))
                dve.wait_ge(vec_in, 16 * 10)
                for st in range(7):
                    if st < 5:
                        j = st
                        T = TQ if j < 4 else TT
                        dve.wait_ge(m["qk_sq"], j + 1)
                        g = qk_g[:, 2 * l + j // 4:2 * l + j // 4 + 1]
                        ts(qn[j][:, 0:T], bank[j % 2][:, 0:T], g, None, ALU.mult).then_inc(m["qk_raw"], 1)
                    j = st - 1
                    if 0 <= j < 5:
                        T = TQ if j < 4 else TT
                        dve.wait_ge(m["root"], j + 2)
                        dve.reciprocal(rstd[:, 0:T], rstd[:, 0:T]).then_inc(m["qk_rstd"], 1)
                        dve.wait_ge(m["qk_rstd"], j + 1)
                        dve.wait_ge(m["qk_raw"], j + 1)
                        tt(qn[j][:, 0:T], qn[j][:, 0:T], rstd[:, 0:T], ALU.mult).then_inc(m["qk_norm"], 1)
                    j = st - 2
                    if 0 <= j < 5:
                        dve.wait_ge(m["qk_norm"], j + 1)
                        if j >= 2:
                            dve.wait_ge(m["roped"], j - 1)
                        tt(tmpB[j % 2][:, 0:S], qn[j][:, 0:S], cos, ALU.mult)
                        dve.wait_ge(m["qk_rot"], j + 1)
                        link(tt(tmpB[j % 2][:, S:TT], bank[4 + j % 2][:, 0:S], sin, ALU.mult))
                        tt(qn[j][:, 0:S], tmpB[j % 2][:, 0:S], tmpB[j % 2][:, S:TT], ALU.add).then_inc(m["roped"], 1)
                for c in range(NC):
                    dve.wait_ge(m["u_sig"], c + 1)
                    a = bank[c % 2][:, 0:TQ].rearrange("p (s t) -> p s t", s=ns)
                    b = tmpA[c % 2][:, 0:TQ].rearrange("p (s t) -> p s t", s=ns)
                    tt(ypad[:, c, 0:ns, PAD:PAD + S], a, b, ALU.mult).then_inc(m["glu"], 1)

                def conv():
                    n = 0
                    for k in range(TAPS):
                            for c in range(3):
                                src = ypad[:, c, 0:ns, k:k + S]
                                dst = acc[c][:, 0:TQ].rearrange("p (s t) -> p s t", s=ns)
                                wk = dwt[:, 124 * l + 4 * k + c:124 * l + 4 * k + c + 1]
                                if k == 0:
                                    dve.wait_ge(m["glu"], c + 1)
                                    i = ts(dst, src, wk, vec2[:, 32 + 4 * l + c:33 + 4 * l + c], ALU.mult, ALU.add)
                                else:
                                    dve.wait_ge(m["conv_step"], n - 2)
                                    i = stt(out=dst, in0=src, scalar=wk, in1=dst, op0=ALU.mult, op1=ALU.add)
                                i.then_inc(m["conv_step"], 1)
                                n += 1
                                yield
                modulation(l, 1)
                modulation(l, 2)
                taps = conv()
                U = units(l)
                per = -(-3 * TAPS // len(U))
                for st in range(len(U)):
                    n = TT - U[st][3] * P
                    dve.wait_ge(m["sc_mm"], st + 1)
                    link(dve.reduce_max(att[:, st:st + 1], bank[st % 2][:, 0:n], AX))
                    ts(att[:, 32 + st:33 + st], att[:, st:st + 1], -HD ** -0.5, None,
                       ALU.mult).then_inc(m["nb_ready"], 1)
                    for _ in range(per):
                        next(taps, None)
                    dve.wait_ge(m["exp_done"], st + 1)
                    link(dve.reciprocal(att[:, 96 + st:97 + st], att[:, 64 + st:65 + st]))
                    if st >= 2:
                        dve.wait_ge(m["pt_mm"], st - 1)
                    ts(diag[st % 2], ident, att[:, 96 + st:97 + st], None, ALU.mult).then_inc(m["diag_ready"], 1)
                for _ in taps:
                    pass
                dve.wait_ge(m["cd_mm"], TAPS)
                ts(acc[3][:, 0:TQ], bank[7][:, 0:TQ], vec2[:, 35 + 4 * l:36 + 4 * l], None,
                   ALU.add).then_inc(m["conv3"], 1)
                dve.wait_ge(m["mean_mm"], 1)
                for c in range(NC):
                    tt(acc[c][:, 0:TQ], acc[c][:, 0:TQ], bank[7][:, 0:TQ], ALU.subtract).then_inc(m["centred"], 1)
                dve.wait_ge(m["centred"], NC)
                dve.wait_ge(m["root"], 7)
                link(dve.reciprocal(rstd[:, 0:TQ], rstd[:, 0:TQ]))
                for c in range(NC):
                    tt(acc[c][:, 0:TQ], acc[c][:, 0:TQ], rstd[:, 0:TQ], ALU.mult).then_inc(m["ln_scaled"], 1)
                if l == 0:
                    piece_rest(0)
                    piece_rest(1)
                for c in range(KT):
                    dve.wait_ge(m["wo_mm"], c + 1)
                    for sg in segs[l]:
                        residual(bank[c % 4], l, c, 16, sg, m["x1"])
                dve.wait_ge(m["x1"], ns * KT)
                dve.wait_ge(m["root"], 8)
                link(dve.reciprocal(rstd[:, 0:TQ], rstd[:, 0:TQ]))
                scale(m, l, 1, "x1", "scaled2", TQ)
                if l == 0:
                    for c in range(KT):
                        dve.wait_ge(hi_ready, h_count(c))
                        tt(h_lo[c], hv[:, c, :], h_hi[c].bitcast(F32), ALU.subtract).then_inc(lo_ready, 1)
                    for n in range(NF):
                        if n < NF - 1:
                            piece_rest(2 * n + 2)
                        else:
                            second_rest(0)
                            second_rest(1)
                        dve.wait_ge(f_silu, n + 1)
                        dve.wait_ge(f_mm, 2 * n + 2)
                        tt(aT[n], aT[n], bank[2 + n % 2][:, :], ALU.mult).then_inc(a_ready, 1)
                        if n < NF - 1:
                            piece_rest(2 * n + 3)
                    for n in range(2, NF):
                        second_rest(n)
                    for c in range(KT):
                        dve.wait_ge(y_mm, c + 1)
                        for sg in (0, 1):
                            residual(bank[(c + 4) % 8], 0, c, 40, sg, x2)
                    dve.wait_ge(x2, 2 * KT)

            dve.wait_ge(tok_mm, 4)
            dve.memset(scr[:, 2048:4096], 0.0)
            dve.memset(ytok, 0.0)
            dve.memset(posm[:, :], BIG)
            link(dve.memset(comb[:, :], 0.0))
            pv = posm[:, :].rearrange("p (e n) -> p e n", n=2)
            cv = comb[:, :].rearrange("p (e n) -> p e n", n=2)
            rev = con[:, REV:REV + NE]
            dve.wait_ge(lg_mm, 1)
            for n in range(2):
                b = 80 * n
                lg, r1, s1, lg2, r2, s2, t1 = (rt[:, b + 8 * i:b + 8 * i + 8] for i in range(7))
                m1, q1, m2, q2, dm, ed, den, g1, g2 = (rt[:, b + i:b + i + 1] for i in (64, 65, 66, 67, 73, 74, 75, 76, 77))
                link(tt(lg, bank[4][:, n * NE:(n + 1) * NE], rb[:, :], ALU.add))
                link(dve.reduce_max(m1, lg, AX))
                link(stt(out=r1, in0=lg, scalar=m1, in1=rev, op0=ALU.is_equal, op1=ALU.mult))
                link(dve.reduce_max(q1, r1, AX))
                link(ts(s1, r1, q1, None, ALU.is_equal))
                link(stt(out=lg2, in0=s1, scalar=-3e38, in1=lg, op0=ALU.mult, op1=ALU.add))
                link(dve.reduce_max(m2, lg2, AX))
                link(stt(out=r2, in0=lg2, scalar=m2, in1=rev, op0=ALU.is_equal, op1=ALU.mult))
                link(dve.reduce_max(q2, r2, AX))
                link(ts(s2, r2, q2, None, ALU.is_equal))
                tt(dm, m2, m1, ALU.subtract).then_inc(dm_ready, 1)
                i = tt(small[:, n * NE:(n + 1) * NE], s1, s2, ALU.add)
                if n == 1:
                    i.then_inc(mask_ready, 1)
                dve.wait_ge(ed_ready, n + 1)
                link(ts(den, ed, 1.0, None, ALU.add))
                link(dve.reciprocal(g1, den))
                link(tt(g2, ed, g1, ALU.mult))
                link(ts(t1, s1, g1, None, ALU.mult))
                link(stt(out=cv[:, 0:NE, n], in0=s2, scalar=g2, in1=t1, op0=ALU.mult, op1=ALU.add))
            dve.wait_ge(mask_ready, 1)
            dve.wait_ge(pos_mm, 1)
            link(dve.reduce_max(rt[:, 78:79], bank[5][:, 2 * NE:3 * NE], AX))
            dve.tensor_copy(most[:, :], rt[:, 78:79]).then_inc(most_ready, 1)
            for n in range(2):
                far = rt[:, 80 * n:80 * n + 8]
                link(ts(far, small[:, n * NE:(n + 1) * NE], -BIG, BIG, ALU.mult, ALU.add))
                i = tt(pv[:, 0:NE, n], bank[5][:, n * NE:(n + 1) * NE], far, ALU.add)
                if n == 0:
                    link(i)
            i.then_inc(pos_ready, 1)
            dve.wait_ge(pos_ready, 1)
            link(dve.memset(cur[:, :], 0.0))
            dve.sem_inc(ea_ready, 2)
            for ahead in (ytok_ready, acc_done, st_mm):
                dve.sem_inc(ahead, 1)

            def select(e, r, step):
                dve.tensor_copy(cur[:, 0:2], pv[:, bass.ds(e, 1), :].rearrange("p a n -> p (a n)")
                                ).then_inc(cur_ready, 1)
                dve.tensor_copy(cur[:, 2:4], cv[:, bass.ds(e, 1), :].rearrange("p a n -> p (a n)")
                                ).then_inc(cur_ready, 1)
                dve.wait_ge(cur_ready, step)
                iota = con[:, IOTA + r * C:IOTA + (r + 1) * C]
                for n in range(2):
                    ts(sel[:, n, :], iota, cur[:, n:n + 1], None, ALU.is_equal)
                    i = ts(selg[:, n, :], iota, cur[:, n:n + 1], cur[:, 2 + n:3 + n], ALU.is_equal, ALU.mult)
                i.then_inc(sel_ready, 1)

            def add(at):
                for pr in range(4):
                    dve.wait_ge(sc_e, at(pr + 1))
                    dst = fT[:, 2 * pr:2 * pr + 2, :]
                    tt(dst, dst, bank[6 + pr % 2][:, :].rearrange("p (c t) -> p c t", c=2),
                       ALU.add).then_inc(acc_done, 1)

            def expert(e, r):
                def at(v, per=NF, steps=NE):
                    return per * e + (per * steps * r + v)

                for n in range(NF):
                    b = n % 2
                    dve.wait_ge(w2hi_ready, at(n + 1))
                    tt(w2_lo[b], w2_row(n), w2_hi[b].bitcast(F32), ALU.subtract)
                    dve.wait_ge(e_silu, at(n + 1))
                    tt(ae[b], ae[b], bank[b][:, C:2 * C], ALU.mult).then_inc(prod, 1)
                    dve.wait_ge(ahi_ready, at(n + 1))
                    tt(ae_lo[b], ae[b], ae_hi[b].bitcast(F32), ALU.subtract).then_inc(ea_ready, 1)
                    if n == 2:
                        add(lambda v: at(v, 4, NE + 1))
                    if n == 12:
                        dve.wait_ge(st_mm, at(2, 1))
                        select(e + 1, r, at(4, 2, NE + 1))

            def experts(r):
                if r:
                    dve.wait_ge(acc_done, 4 * (NE + 1) * r + 1)
                dve.memset(sgT, 0.0).then_inc(sgt_zero, 1)
                select(0, r, 2 * (NE + 1) * r + 2)
                with dve.Fori(0, NE) as e:
                    expert(e, r)
                add(lambda v: 4 * (NE + 1) * r + 4 * NE + v)
                dve.wait_ge(acc_done, 4 * (NE + 1) * (r + 1) + 1)

            rounds(dve, experts)
            for c in range(KT):
                x = xv[:, c, 0:S]
                stt(out=x, in0=fT[:, c, :], scalar=mods[1][:, 40 + c, 0:1], in1=x,
                    op0=ALU.mult, op1=ALU.add).then_inc(xf, 1)
            dve.wait_ge(xf, KT)
            dve.wait_ge(rootf, 1)
            link(dve.reciprocal(frstd, frstd))
            for c in range(KT):
                stt(out=hv[:, c, 0:S], in0=xv[:, c, 0:S], scalar=vec1[:, 112 + c:113 + c], in1=frstd,
                    op0=ALU.mult, op1=ALU.mult).then_inc(outn, 1)


def tables():
    import numpy as np
    i = np.arange(P)
    m = {
        "ident": np.eye(P),
        "mean_d": np.full((P, P), 1 / D),
        "mean_head": (i[:, None] // HD == i[None, :] // HD) / HD,
        "mean_conv": np.full((P, P), 1 / 512),
        "rot": np.where((i[:, None] ^ 1) == i[None, :], np.where(i[None, :] % 2 == 0, -1.0, 1.0), 0.0),
        "halves": (i[:, None] + HD) % P == i[None, :],
        "before": i[:, None] < i[None, :],
        "ones": np.ones((P, P)),
    }
    tok = np.arange(S)
    inv = (np.float32(10000.0) ** (-np.arange(0, 32, 2, dtype=np.float32) / np.float32(32))).astype(np.float32)
    ang = np.concatenate([(tok // 64).astype(np.float32)[:, None] * inv,
                          (tok % 64).astype(np.float32)[:, None] * inv], axis=-1)
    pair = (i % HD) // 2
    cols = [np.asarray(m[n], np.float32) for n in CONSTS]
    cols += [np.cos(ang).T[pair].astype(np.float32), np.sin(ang).T[pair].astype(np.float32)]
    cols += [np.broadcast_to(np.arange(ROUNDS * C, dtype=np.float32), (P, ROUNDS * C)),
             np.broadcast_to(np.arange(NE, 0, -1, dtype=np.float32), (P, NE))]
    return np.ascontiguousarray(np.concatenate(cols, axis=1), dtype=np.float32)


_INS = ["x", "c", "ctx", "c_ctx", "w_ada", "b_ada", "norm1_g", "w_in", "q_norm_g", "k_norm_g", "dw_w", "dw_b",
        "conv_ln_g", "conv_ln_b", "w_out", "norm2_g", "ffn_w1", "ffn_w3", "ffn_w2", "router_w", "router_b",
        "exp_w1", "exp_w3", "exp_w2", "final_g"]


def kernel(**inputs):
    import numpy as np
    import concourse.bacc as bacc
    from concourse.bass_utils import run_bass_kernel_spmd as run

    nc = bacc.Bacc("TRN2", target_bir_lowering=False, num_devices=1)
    arrays, t = {}, {}
    host = {n: np.ascontiguousarray(inputs[n]) for n in _INS}
    host["constants"] = tables()
    for name, a in host.items():
        arrays[f"in_{name}"] = a
        t[name] = nc.dram_tensor(f"in_{name}", a.shape, F32, kind="ExternalInput").ap()
    out = nc.dram_tensor("out", [1, S, D], F32, kind="ExternalOutput").ap()
    backbone(nc, t, out)
    r = run(nc, [arrays], core_ids=[0])
    return r.results[0]["out"]
```
